# Optimizing a Trainium2 kernel written in Bass

```python
import math
import jax, jax.numpy as jnp
from jax import lax
import numpy as np

D_MODEL = 1024
BATCH = 1
SEQ = 512
DEPTH = 1
DEC_BATCH = 8
DEC_SEQ = 1
PAST_LEN = 4096
PAGE_SIZE = 128

NSA_HEADS = 8
NSA_KV_HEADS = 2
NSA_GROUP = NSA_HEADS // NSA_KV_HEADS
NSA_HEAD_DIM = 64
NSA_WIDTH = NSA_HEADS * NSA_HEAD_DIM
NSA_KV_WIDTH = NSA_KV_HEADS * 2 * NSA_HEAD_DIM
ROT_DIM = NSA_HEAD_DIM // 4
ROPE_THETA = 500000.0
CMP_BLOCK = 32
SEL_BLOCK = 64
SEL_RATIO = SEL_BLOCK // CMP_BLOCK
N_SELECT = 16
WINDOW = 512
NSA_QBLOCK = 32
NSA_SCALE = NSA_HEAD_DIM ** -0.5

MLA_HEADS = 8
MLA_Q_LORA = 384
MLA_KV_LORA = 256
MLA_NOPE = 64
MLA_ROPE = 32
MLA_V = 64
MLA_WIDTH = MLA_HEADS * MLA_V
MLA_ROPE_THETA = 10000.0
MLA_QBLOCK = 128
MLA_SCALE = (MLA_NOPE + MLA_ROPE) ** -0.5

RMS_EPS = 1e-6
NEG_INF = -1e30
FORCE_SCORE = 1e4

IN_SPLITS = (NSA_WIDTH, NSA_KV_WIDTH, NSA_KV_WIDTH, NSA_KV_WIDTH, 3 * NSA_HEADS, NSA_WIDTH,
             MLA_Q_LORA, MLA_KV_LORA, MLA_ROPE, MLA_WIDTH, D_MODEL, D_MODEL)
IN_WIDTH = sum(IN_SPLITS)
IN_OFFSETS = tuple(int(v) for v in np.cumsum(IN_SPLITS)[:-1])

kernel_name = "hybrid_nsa_mla_gated_decode_step"

def _rmsnorm(x, g):
    x32 = x.astype(jnp.float32)
    y = x32 * lax.rsqrt(jnp.mean(x32 * x32, axis=-1, keepdims=True) + RMS_EPS)
    return (y * g.astype(jnp.float32)).astype(x.dtype)

def _rope(x, pos, theta):
    half = x.shape[-1] // 2
    inv = 1.0 / (jnp.float32(theta) ** (jnp.arange(half, dtype=jnp.float32) / half))
    ang = pos.astype(jnp.float32)[:, None] * inv[None, :]
    if x.ndim == 4:
        ang = ang[:, None, :]
    cos, sin = jnp.cos(ang), jnp.sin(ang)
    x1 = x[..., :half].astype(jnp.float32)
    x2 = x[..., half:].astype(jnp.float32)
    return jnp.concatenate([x1 * cos - x2 * sin, x1 * sin + x2 * cos], axis=-1).astype(x.dtype)

def _partial_rope(x, pos):
    return jnp.concatenate([_rope(x[..., :ROT_DIM], pos, ROPE_THETA), x[..., ROT_DIM:]], axis=-1)

def _rope_kv(kv, pos):
    return jnp.stack([_partial_rope(kv[..., 0, :], pos), kv[..., 1, :]], axis=-2)

def _masked_softmax(s, mask):
    s = jnp.where(mask, s.astype(jnp.float32), NEG_INF)
    p = jax.nn.softmax(s, axis=-1)
    return jnp.where(mask, p, 0.0)

def _to_blocks(a, qb):
    b, t = a.shape[:2]
    return a.reshape(b, t // qb, qb, *a.shape[2:]).swapaxes(0, 1)

def _from_blocks(a):
    a = a.swapaxes(0, 1)
    return a.reshape(a.shape[0], a.shape[1] * a.shape[2], *a.shape[3:])

def _compress(kv, pe_cmp):
    b, s = kv.shape[:2]
    s_pad = -(-s // SEL_BLOCK) * SEL_BLOCK
    kv = jnp.pad(kv, ((0, 0), (0, s_pad - s), (0, 0), (0, 0), (0, 0)))
    blocks = kv.reshape(b, s_pad // CMP_BLOCK, CMP_BLOCK, NSA_KV_HEADS, 2, NSA_HEAD_DIM)
    c = jnp.mean(blocks + pe_cmp[None, None], axis=2)
    return c[..., 0, :], c[..., 1, :]

def _nsa_attend(q, q_rot, g, t, kc, vc, gather, kvw, pos_w):
    b, nq = q.shape[:2]
    qg = q.reshape(b, nq, NSA_KV_HEADS, NSA_GROUP, NSA_HEAD_DIM)
    qr = q_rot.reshape(b, nq, NSA_KV_HEADS, NSA_GROUP, NSA_HEAD_DIM)
    nc = kc.shape[1]
    nb = nc // SEL_RATIO
    s_c = jnp.einsum('bqgrd,bngd->bqgrn', qg, kc) * NSA_SCALE
    end_c = (jnp.arange(nc) + 1) * CMP_BLOCK - 1
    mask_c = (end_c[None, :] <= t[:, None])[None, :, None, None, :]
    p_c = _masked_softmax(s_c, mask_c)
    o_c = jnp.einsum('bqgrn,bngd->bqgrd', p_c.astype(vc.dtype), vc)
    imp = p_c.sum(axis=3).reshape(b, nq, NSA_KV_HEADS, nb, SEL_RATIO).sum(-1)
    j = jnp.arange(nb)
    valid = (j[None, :] * SEL_BLOCK <= t[:, None])[None, :, None, :]
    forced = ((j[None, :] == (t // SEL_BLOCK)[:, None]) | (j[None, :] == 0))[None, :, None, :]
    score = jnp.where(forced, FORCE_SCORE, jnp.where(valid, imp, -FORCE_SCORE))
    top, idx = lax.top_k(score, min(N_SELECT, nb))
    pos_sel = idx[..., None] * SEL_BLOCK + jnp.arange(SEL_BLOCK)
    k_sel, v_sel = gather(pos_sel)
    n_sel = pos_sel.shape[3]
    s_s = jnp.einsum('bqgrd,bqgkld->bqgrkl', qr, k_sel) * NSA_SCALE
    mask_s = (top > -1.0)[..., None] & (pos_sel <= t[None, :, None, None, None])
    p_s = _masked_softmax(s_s.reshape(b, nq, NSA_KV_HEADS, NSA_GROUP, n_sel * SEL_BLOCK),
                          mask_s.reshape(b, nq, NSA_KV_HEADS, 1, n_sel * SEL_BLOCK))
    p_s = p_s.reshape(s_s.shape)
    o_s = jnp.einsum('bqgrkl,bqgkld->bqgrd', p_s.astype(v_sel.dtype), v_sel)
    s_w = jnp.einsum('bqgrd,bsgd->bqgrs', qr, kvw[..., 0, :]) * NSA_SCALE
    dist = t[:, None] - pos_w[None, :]
    mask_w = ((dist >= 0) & (dist <= WINDOW) & (pos_w[None, :] >= 0))[None, :, None, None, :]
    p_w = _masked_softmax(s_w, mask_w)
    o_w = jnp.einsum('bqgrs,bsgd->bqgrd', p_w.astype(kvw.dtype), kvw[..., 1, :])
    gg = g.reshape(b, nq, NSA_KV_HEADS, NSA_GROUP, 3)
    o = gg[..., 0:1] * o_c + gg[..., 1:2] * o_s + gg[..., 2:3] * o_w
    return o.reshape(b, nq, NSA_WIDTH)

def _mla_attend(q_lat, q_pe, t, c, kr, pos_k):
    s = (jnp.einsum('bqhc,bsc->bhqs', q_lat, c) + jnp.einsum('bqhr,bsr->bhqs', q_pe, kr)) * MLA_SCALE
    mask = (pos_k[None, :] <= t[:, None])[None, None]
    p = _masked_softmax(s, mask)
    return jnp.einsum('bhqs,bsc->bqhc', p.astype(c.dtype), c)

def _project_in(x, pos, norm_pre, w_in, q_norm, w_q_up, kv_norm, w_kv_up):
    b, t = x.shape[:2]
    xn = _rmsnorm(x, norm_pre)
    (qa, kvc, kvs, kvw, gn, ga, qd, kvd, krp, gb, ma, mb) = jnp.split(xn @ w_in, IN_OFFSETS, axis=-1)
    kv_shape = (b, t, NSA_KV_HEADS, 2, NSA_HEAD_DIM)
    q = qa.reshape(b, t, NSA_HEADS, NSA_HEAD_DIM)
    nsa = (q, _partial_rope(q, pos), jax.nn.sigmoid(gn.reshape(b, t, NSA_HEADS, 3)),
           kvc.reshape(kv_shape), _rope_kv(kvs.reshape(kv_shape), pos), _rope_kv(kvw.reshape(kv_shape), pos))
    qh = jnp.einsum('btc,chd->bthd', _rmsnorm(qd, q_norm), w_q_up)
    q_pe = _rope(qh[..., MLA_NOPE:], pos, MLA_ROPE_THETA)
    q_lat = jnp.einsum('bthn,chn->bthc', qh[..., :MLA_NOPE], w_kv_up[..., :MLA_NOPE])
    c = _rmsnorm(kvd, kv_norm)
    kr = _rope(krp, pos, MLA_ROPE_THETA)
    return nsa, (q_lat, q_pe, c, kr), (ga, gb, ma, mb)

def _merge_out(x, o_a, o_lat, gates, w_kv_up, w_proj_a, w_proj_b, w_out, norm_post):
    ga, gb, ma, mb = gates
    b, t = x.shape[:2]
    o_b = jnp.einsum('bqhc,chv->bqhv', o_lat, w_kv_up[..., MLA_NOPE:]).reshape(b, t, MLA_WIDTH)
    pa = (o_a * jax.nn.silu(ga)) @ w_proj_a
    pb = (o_b * jax.nn.silu(gb)) @ w_proj_b
    h = jax.nn.sigmoid(ma) * pa + jax.nn.sigmoid(mb) * pb
    return x + _rmsnorm(h @ w_out, norm_post)

def _prompt_layer(x, norm_pre, w_in, pe_cmp, q_norm, w_q_up, kv_norm, w_kv_up,
                  w_proj_a, w_proj_b, w_out, norm_post):
    b, t = x.shape[:2]
    pos = jnp.arange(t)
    nsa, mla, gates = _project_in(x, pos, norm_pre, w_in, q_norm, w_q_up, kv_norm, w_kv_up)
    q, q_rot, g, kvc, kvs, kvw = nsa
    kc, vc = _compress(kvc, pe_cmp)
    kvw_pad = jnp.pad(kvw, ((0, 0), (WINDOW, 0), (0, 0), (0, 0), (0, 0)))
    b_i = jnp.arange(b)[:, None, None, None, None]
    g_i = jnp.arange(NSA_KV_HEADS)[None, None, :, None, None]

    def gather(pos_sel):
        p = jnp.clip(pos_sel, 0, t - 1)
        return kvs[b_i, p, g_i, 0], kvs[b_i, p, g_i, 1]

    def nsa_block(args):
        i, qb, qrb, gbk = args
        s0 = i * NSA_QBLOCK
        tq = s0 + jnp.arange(NSA_QBLOCK)
        kvw_b = lax.dynamic_slice_in_dim(kvw_pad, s0, WINDOW + NSA_QBLOCK, axis=1)
        pos_w = s0 - WINDOW + jnp.arange(WINDOW + NSA_QBLOCK)
        return _nsa_attend(qb, qrb, gbk, tq, kc, vc, gather, kvw_b, pos_w)

    o_a = _from_blocks(lax.map(nsa_block, (jnp.arange(t // NSA_QBLOCK), _to_blocks(q, NSA_QBLOCK),
                                           _to_blocks(q_rot, NSA_QBLOCK), _to_blocks(g, NSA_QBLOCK))))
    q_lat, q_pe, c, kr = mla

    def mla_block(args):
        i, ql, qp = args
        tq = i * MLA_QBLOCK + jnp.arange(MLA_QBLOCK)
        return _mla_attend(ql, qp, tq, c, kr, pos)

    o_lat = _from_blocks(lax.map(mla_block, (jnp.arange(t // MLA_QBLOCK), _to_blocks(q_lat, MLA_QBLOCK),
                                             _to_blocks(q_pe, MLA_QBLOCK))))
    y = _merge_out(x, o_a, o_lat, gates, w_kv_up, w_proj_a, w_proj_b, w_out, norm_post)
    win_keep = min(WINDOW, t)
    return y, kvc, kvs, c, kr, kvw[:, t - win_keep:]

def _sample_layer(x, l, cache_nsa_cmp, cache_nsa_slc, cache_mla_latent, cache_mla_krope, state_win,
                  page_table, norm_pre, w_in, pe_cmp, q_norm, w_q_up, kv_norm, w_kv_up,
                  w_proj_a, w_proj_b, w_out, norm_post):
    b, s_new = x.shape[:2]
    n_pages = page_table.shape[1]
    page = cache_nsa_cmp.shape[2]
    past = n_pages * page
    pos = past + jnp.arange(s_new)
    nsa, mla, gates = _project_in(x, pos, norm_pre, w_in, q_norm, w_q_up, kv_norm, w_kv_up)
    q, q_rot, g, kvc, kvs, kvw = nsa
    cmp_past = cache_nsa_cmp[l, page_table].reshape(b, past, NSA_KV_HEADS, 2, NSA_HEAD_DIM)
    kc, vc = _compress(jnp.concatenate([cmp_past, kvc], axis=1), pe_cmp)
    b_i = jnp.arange(b)[:, None, None, None, None]
    g_i = jnp.arange(NSA_KV_HEADS)[None, None, :, None, None]

    def gather(pos_sel):
        in_past = (pos_sel < past)[..., None]
        phys = page_table[b_i, jnp.clip(pos_sel // page, 0, n_pages - 1)]
        off = pos_sel % page
        p_new = jnp.clip(pos_sel - past, 0, s_new - 1)
        k = jnp.where(in_past, cache_nsa_slc[l, phys, off, g_i, 0], kvs[b_i, p_new, g_i, 0])
        v = jnp.where(in_past, cache_nsa_slc[l, phys, off, g_i, 1], kvs[b_i, p_new, g_i, 1])
        return k, v

    win_len = state_win.shape[1]
    kvw_all = jnp.concatenate([state_win, kvw], axis=1)
    pos_w = past - win_len + jnp.arange(win_len + s_new)
    o_a = _nsa_attend(q, q_rot, g, pos, kc, vc, gather, kvw_all, pos_w)
    q_lat, q_pe, c, kr = mla
    c_all = jnp.concatenate([cache_mla_latent[l, page_table].reshape(b, past, MLA_KV_LORA), c], axis=1)
    kr_all = jnp.concatenate([cache_mla_krope[l, page_table].reshape(b, past, MLA_ROPE), kr], axis=1)
    o_lat = _mla_attend(q_lat, q_pe, pos, c_all, kr_all, jnp.arange(past + s_new))
    y = _merge_out(x, o_a, o_lat, gates, w_kv_up, w_proj_a, w_proj_b, w_out, norm_post)
    return y, kvc, kvs, c, kr, kvw_all[:, s_new:]

def setup_inputs(seed: int = 0) -> dict:
    key = jax.random.key(seed)
    ks = jax.random.split(key, 24)
    n_pages = PAST_LEN // PAGE_SIZE
    n_used = DEC_BATCH * n_pages
    n_phys = n_used + max(1, n_used // 4)
    win_len = min(WINDOW, PAST_LEN)

    def nrm(k, shape, scale):
        return scale * jax.random.normal(k, shape, jnp.float32)

    kvrow = (NSA_KV_HEADS, 2, NSA_HEAD_DIM)
    return {
        "x_prompt": nrm(ks[0], (BATCH, SEQ, D_MODEL), 1.0),
        "x_sample": nrm(ks[1], (DEC_BATCH, DEC_SEQ, D_MODEL), 1.0),
        "cache_nsa_cmp": nrm(ks[2], (DEPTH, n_phys, PAGE_SIZE) + kvrow, 1.0),
        "cache_nsa_slc": nrm(ks[3], (DEPTH, n_phys, PAGE_SIZE) + kvrow, 1.0),
        "cache_mla_latent": nrm(ks[4], (DEPTH, n_phys, PAGE_SIZE, MLA_KV_LORA), 1.0),
        "cache_mla_krope": nrm(ks[5], (DEPTH, n_phys, PAGE_SIZE, MLA_ROPE), 1.0),
        "state_nsa_win": nrm(ks[6], (DEPTH, DEC_BATCH, win_len) + kvrow, 1.0),
        "page_table": jax.random.permutation(ks[7], n_phys)[:n_used].reshape(DEC_BATCH, n_pages).astype(jnp.int32),
        "norm_pre": 1.0 + nrm(ks[8], (DEPTH, D_MODEL), 0.05),
        "w_in": nrm(ks[9], (DEPTH, D_MODEL, IN_WIDTH), D_MODEL ** -0.5),
        "pe_cmp": nrm(ks[10], (DEPTH, CMP_BLOCK) + kvrow, 0.1),
        "q_norm": 1.0 + nrm(ks[11], (DEPTH, MLA_Q_LORA), 0.05),
        "w_q_up": nrm(ks[12], (DEPTH, MLA_Q_LORA, MLA_HEADS, MLA_NOPE + MLA_ROPE), MLA_Q_LORA ** -0.5),
        "kv_norm": 1.0 + nrm(ks[13], (DEPTH, MLA_KV_LORA), 0.05),
        "w_kv_up": nrm(ks[14], (DEPTH, MLA_KV_LORA, MLA_HEADS, MLA_NOPE + MLA_V), MLA_KV_LORA ** -0.5),
        "w_proj_a": nrm(ks[15], (DEPTH, NSA_WIDTH, D_MODEL), NSA_WIDTH ** -0.5),
        "w_proj_b": nrm(ks[16], (DEPTH, MLA_WIDTH, D_MODEL), MLA_WIDTH ** -0.5),
        "w_out": nrm(ks[17], (DEPTH, D_MODEL, D_MODEL), D_MODEL ** -0.5),
        "norm_post": 1.0 + nrm(ks[18], (DEPTH, D_MODEL), 0.05),
    }

def reference(x_prompt, x_sample, cache_nsa_cmp, cache_nsa_slc, cache_mla_latent, cache_mla_krope,
              state_nsa_win, page_table, norm_pre, w_in, pe_cmp, q_norm, w_q_up, kv_norm, w_kv_up,
              w_proj_a, w_proj_b, w_out, norm_post):
    hp, hs = x_prompt, x_sample
    new_p, new_s = [], []
    for l in range(DEPTH):
        w = (norm_pre[l], w_in[l], pe_cmp[l], q_norm[l], w_q_up[l], kv_norm[l], w_kv_up[l],
             w_proj_a[l], w_proj_b[l], w_out[l], norm_post[l])
        hp, *sp = _prompt_layer(hp, *w)
        hs, *ss = _sample_layer(hs, l, cache_nsa_cmp, cache_nsa_slc, cache_mla_latent, cache_mla_krope,
                                state_nsa_win[l], page_table, *w)
        new_p.append(sp)
        new_s.append(ss)
    new_cmp_p = jnp.stack([s[0] for s in new_p])
    new_slc_p = jnp.stack([s[1] for s in new_p])
    new_lat_p = jnp.stack([s[2] for s in new_p])
    new_krope_p = jnp.stack([s[3] for s in new_p])
    new_win_p = jnp.stack([s[4] for s in new_p])
    new_cmp_s = jnp.stack([s[0] for s in new_s])
    new_slc_s = jnp.stack([s[1] for s in new_s])
    new_lat_s = jnp.stack([s[2] for s in new_s])
    new_krope_s = jnp.stack([s[3] for s in new_s])
    new_win_s = jnp.stack([s[4] for s in new_s])
    return (hp, hs, new_cmp_p, new_slc_p, new_lat_p, new_krope_p, new_win_p,
            new_cmp_s, new_slc_s, new_lat_s, new_krope_s, new_win_s)


_drawn_inputs = setup_inputs


def setup_inputs(seed=0):
    import zlib

    import numpy as np

    out = dict(_drawn_inputs(seed))
    spreads = {}
    factors = {}
    for name, (base, spread) in spreads.items():
        noise = np.random.default_rng([zlib.crc32(name.encode()), seed]).standard_normal(out[name].shape)
        drawn = base * np.exp(spread * noise) if base else spread * noise
        out[name] = __import__('jax').numpy.asarray(drawn.astype(out[name].dtype))
    for name, factor in factors.items():
        out[name] = (out[name] * factor).astype(out[name].dtype)
    return out
```

```python
from contextlib import ExitStack

import numpy as np

import concourse.bass as bass
from concourse import mybir

F32 = mybir.dt.float32
BF16 = mybir.dt.bfloat16
I32 = mybir.dt.int32
U32 = mybir.dt.uint32
ALU = mybir.AluOpType
ACT = mybir.ActivationFunctionType
AX_X = mybir.AxisListType.X

P = 128
D_MODEL = 1024
SEQ = 512
DEC = 8
PAST = 4096
PAGE = 128
N_PAGES = PAST // PAGE
HEADS, KVH, HD = 8, 2, 64
ROT = HD // 4
CMP_BLOCK, SEL_BLOCK, N_SELECT = 32, 64, 16
WINDOW = 512
Q_LORA, KV_LORA, NOPE, ROPE_D, V_D = 384, 256, 64, 32, 64
EPS = 1e-6
NEG = -1e30
FORCE = 1e4
NSA_SCALE = HD ** -0.5
MLA_SCALE = (NOPE + ROPE_D) ** -0.5
TILES = SEQ // P
KM = D_MODEL // P
TOK = SEQ + DEC

C_Q, C_KS, C_KW, C_VS, C_VW = 0, 512, 640, 768, 896
C_KC, C_VC, C_GN, C_QD, C_CD, C_KR = 1024, 1152, 1280, 1304, 1688, 1944
W_ATTN = 1976
NG = 4
GW = W_ATTN // NG
JOB = 4096
RING = 3
SMALL = 1076

CST = {}


def constants():
    cols = []

    def put(name, a):
        full = np.zeros((P, a.shape[1]), np.float32)
        full[: a.shape[0]] = a
        CST[name] = (sum(c.shape[1] for c in cols), a.shape[0], a.shape[1])
        cols.append(full)

    p = np.arange(P)
    put("ident", np.eye(P, dtype=np.float32))
    pos = np.arange(SEQ, dtype=np.float32)

    def angles(half, theta):
        inv = (np.float32(1.0) / (np.float32(theta) ** (np.arange(half, dtype=np.float32) / np.float32(half)))).astype(np.float32)
        prompt = (pos[:, None] * inv[None]).astype(np.float32)
        dec = (np.float32(PAST) * inv).astype(np.float32)
        return prompt, dec

    def table(half, theta, fn):
        prompt, dec = angles(half, theta)
        t = fn(prompt.astype(np.float64)).astype(np.float32).reshape(TILES, P, half).transpose(1, 0, 2)
        d = np.broadcast_to(fn(dec.astype(np.float64)).astype(np.float32)[None, None], (P, 1, half))
        return np.concatenate([t, d], 1).reshape(P, -1)

    put("cos8", table(8, 500000.0, np.cos))
    put("sin8", table(8, 500000.0, np.sin))
    put("cos16", table(16, 10000.0, np.cos))
    put("sin16", table(16, 10000.0, np.sin))
    prompt, dec = angles(16, 10000.0)
    ang = np.concatenate([prompt, np.broadcast_to(dec[None], (DEC, 16))], 0).astype(np.float64).T
    rt = np.zeros((P, TOK), np.float32)
    rt[64:80] = rt[80:96] = np.cos(ang)
    rt[96:112] = -np.sin(ang)
    rt[112:128] = np.sin(ang)
    put("causal", np.where(p[None, :] <= p[:, None], 0.0, NEG).astype(np.float32))
    put("pool", np.where(p[:, None] // 4 == np.arange(32)[None], 1.0 / CMP_BLOCK, 0.0).astype(np.float32))
    put("onesmean", np.full((CMP_BLOCK, P), 1.0 / CMP_BLOCK, np.float32))
    n = np.arange(16)
    pw = np.zeros((P, TILES, 16), np.float32)
    for t in range(TILES):
        pw[:, t] = np.where(4 * t + p[:, None] // CMP_BLOCK == n[None], 1.0 / CMP_BLOCK, 0.0)
    put("poolp", pw.reshape(P, -1))
    cm = np.zeros((P, TILES, 16), np.float32)
    for t in range(TILES):
        cm[:, t] = (n[None] + 1) * CMP_BLOCK - 1 <= (t * P + p)[:, None]
    put("cmask01", cm.reshape(P, -1))
    put("cmaskneg", np.where(cm > 0, 0.0, NEG).astype(np.float32).reshape(P, -1))
    put("rep16", (np.arange(16)[:, None] == p[None] % 16).astype(np.float32))
    put("headsel16", (p[:, None] // 16 == np.arange(8)[None]).astype(np.float32))
    put("exp8", (np.arange(8)[:, None] == p[None] // 16).astype(np.float32))
    put("exp4", (np.arange(4)[:, None] == p[None] // 32).astype(np.float32))
    put("exp16", (np.arange(16)[:, None] == p[None] // 8).astype(np.float32))
    put("mod", np.stack([p % 16, p % 32, p % 8], 1).astype(np.float32))
    r16 = np.arange(16)
    put("selbase", ((np.arange(64) % 2) * 16)[None, :] + ((r16 % 2) * 8)[:, None] + np.zeros((16, 64), np.float32))
    put("iota64", np.broadcast_to(np.arange(64, dtype=np.float32), (16, 64)))
    put("force0", np.broadcast_to(np.where(np.arange(64) == 0, FORCE, 0.0).astype(np.float32), (16, 64)))
    r64 = np.arange(64)
    put("headsum", (r64[:, None] // 4 == r16[None]).astype(np.float32))
    put("b2bh", (np.arange(8)[:, None] == r64[None] // 8).astype(np.float32))
    put("own3", np.repeat((r64[:, None] % 8 == np.arange(8)[None]).astype(np.float32), 3, axis=1))
    put("ggrp", np.stack([(r64 % 8) < 4, (r64 % 8) >= 4], 1).astype(np.float32))
    put("ggrp32", np.stack([(p % 32) < 4, ((p % 32) >= 4) & ((p % 32) < 8)], 1).astype(np.float32))
    ss = np.zeros((P, 4, 64), np.float32)
    for r in range(4):
        for q in range(P):
            j, hh = q // 32, q % 32
            if hh < 4:
                ss[q, r, (2 * r + j // 2) * 8 + (j % 2) * 4 + hh] = 1
    put("selS", ss.reshape(P, -1))
    sw = np.zeros((P, 2, 64), np.float32)
    for r in range(2):
        for q in range(P):
            if q % 32 < 8:
                sw[q, r, (4 * r + q // 32) * 8 + q % 32] = 1
    put("selW", sw.reshape(P, -1))
    st = np.zeros((64, 8, 8), np.float32)
    for h in range(8):
        for b in range(8):
            st[b * 8 + h, h, b] = 1
    put("selT", st.reshape(64, -1))
    put("selH", ((p[:, None] % 32) == np.arange(8)[None]).astype(np.float32))
    ms = np.full((P, 4, 8), NEG, np.float32)
    mw = np.full((P, 2, 8), NEG, np.float32)
    mm = np.full((P, 8, 8), NEG, np.float32)
    for q in range(P):
        j = q // 32
        for r in range(4):
            ms[q, r, 2 * r + j // 2] = 0
        for r in range(2):
            mw[q, r, 4 * r + j] = 0
        if j == 0:
            for b in range(8):
                mm[q, b, b] = 0
    put("newS", ms.reshape(P, -1))
    put("newW", mw.reshape(P, -1))
    put("newM", mm.reshape(P, -1))
    put("ropeT", rt)
    return np.ascontiguousarray(np.concatenate(cols, 1))


CONST = constants()
NC_CST = CST["ropeT"][0]


def build(nc, t):
    ctx = ExitStack()
    with ctx:
        def sb(name, words, dt=F32):
            return ctx.enter_context(nc.sbuf_tensor(name, [P, words], dt))

        class Sems:

            def __init__(self):
                self.made = {}

            def __getitem__(self, name):
                if name not in self.made:
                    self.made[name] = ctx.enter_context(nc.semaphore(name))
                return self.made[name]

        S = Sems()

        cst = sb("cst", NC_CST)
        projP = sb("projP", TILES * W_ATTN)
        projD = sb("projD", W_ATTN)
        ring = sb("ring", RING * JOB)
        W = sb("W", NG * 8 * GW)
        XG = sb("XG", KM * TOK)
        OA = sb("OA", 5 * 512)
        OB = sb("OB", 5 * 512)
        VV = sb("VV", TILES * 256)
        KRR = sb("KRR", RING * 256)
        identb = sb("identb", P, BF16)
        causb = sb("causb", P, BF16)
        idxi = sb("idxi", 32 + 64 + 16, I32)
        pti = sb("pti", 32 + 64 + 32 + 256, I32)
        sm = sb("sm", SMALL)
        bank = [ctx.enter_context(nc.psum_tensor(f"bank{i}", [P, 512], F32)) for i in range(8)]

        def C(name, lo=0, width=None, rows=P):
            off, _, w = CST[name]
            return cst[0:rows, off + lo:off + (w if width is None else lo + width)]

        class Carve:
            def __init__(self, region, words, start=0):
                self.r, self.words, self.at = region, words, start

            def __call__(self, words):
                a = self.at
                self.at += words
                assert self.at <= self.words, (self.at, self.words)
                return self.r[:, a:a + words]

        pP = projP[:, :].rearrange("p (t c) -> p t c", t=TILES)
        c_ = Carve(sm, SMALL)
        normpre, qnorm = c_(8), c_(3)
        ss5, v5, rs5, rt5 = c_(5), c_(5), c_(5), c_(5)
        ss10, v10, rs10, rt10 = c_(10), c_(10), c_(10), c_(10)
        ssz, vz, rsz, rtz = c_(10), c_(5), c_(5), c_(5)
        gsig = c_(120)
        NMp, RSp, CFp = c_(96), c_(96), c_(96)
        NMd, RSd, ALd, LD = c_(56), c_(56), c_(56), c_(56)
        cTn = c_(16)
        krn = c_(8)
        KnS = c_(16)
        KnW = c_(8)
        g3, tcol, lnv = c_(3), c_(8), c_(16)
        od1, oC64, oS64, qmd = c_(64), c_(64), c_(64), c_(64)
        slot = [ring[:, n * JOB:(n + 1) * JOB] for n in range(RING)]
        c_ = Carve(projP, 7904)
        xtok, xdec, sqs = c_(4096), c_(1024), c_(1024)
        c_ = Carve(OB, 2560)
        KcT, VcD, mpe, petile = c_(8 * P), c_(8 * P), c_(256), c_(256)
        c_ = Carve(OA, 2560)
        QZraw, ctmp, PcZ, scD, pcD = c_(512), c_(256), c_(512), c_(P), c_(P)
        impD, imp2, m16, f16, R16, RT16, rowb, ptf = c_(64), c_(64), c_(16), c_(16), c_(16), c_(16), c_(64), c_(128)
        bh24, nmc, rsc, rcc, kvn = c_(24), c_(1), c_(1), c_(1), c_(256)
        i16 = sb("i16", 16, U32)
        c_ = Carve(W, 15808)
        qrT, KT2, qmT, kmT, vm = c_(2048), c_(2048), c_(4096), c_(4096), c_(2048)
        QZw, QL, PTd = c_(256), c_(512), c_(512)
        qTraw = qmT[:, 0:2048]
        tmpA, tA, tB, sq2, VcBD = kmT[:, 0:1536], kmT[:, 1536:2048], kmT[:, 2048:2560], kmT[:, 3584:4096], PTd
        c_ = Carve(XG, 4160)
        qdnT, cT, Sc, pcP, kcBD, vcs, cs32 = c_(3 * TOK), c_(2 * TOK), c_(512), c_(512), c_(64), c_(P), c_(96)
        c_ = Carve(projP, 7904)
        OF, QZs, QR = c_(2048), c_(1024), c_(1024)
        Pb = [c_(512) for _ in range(3)]
        PTb = [c_(512) for _ in range(2)]
        Pd, owS, owW = c_(512), c_(256), c_(256)
        mrg, coefT, Wsel = PTb[0][:, 0:448], PTb[1][:, 0:8], PTb[1][:, 8:72]
        KTs = OF
        c_ = Carve(W, 15808)
        oT, H, sA, sB = c_(8 * TOK), c_(5 * D_MODEL), c_(5 * 512), c_(5 * 512)
        hT = projP[:, 0:8 * TOK]
        ztmp = projP[:, 4352:4352 + 1024]

        N_STORED = 16 * 8
        J_CMP, J_W1, J_W2, J_WIN, J_SLC, J_MLA = 0, 16, 17, 18, 20, 24
        J_GA, J_GB, J_GATE, J_WO = 56, 57, 58, 64
        N_JOBS = 66
        last_chunk, last_z = {}, {}

        def dmas_of(n):
            if n < J_W1:
                return 2
            if n < J_WIN:
                return 2 + n - J_W1
            if n < J_MLA:
                return 4
            if n < J_GA:
                return 8
            return 2 if n in (60, 63) else 1

        def slot_sem(n):
            gathered = n < J_W1 or J_SLC <= n < J_MLA
            return f"slot{n % RING}_" + ("gathered" if gathered else "landed")

        landed, total = {}, {}
        for n in range(N_JOBS):
            total[slot_sem(n)] = total.get(slot_sem(n), 0) + 16 * dmas_of(n)
            landed[n] = total[slot_sem(n)]

        def job(n):
            return slot[n % RING]

        def job_landed(eng, n):
            eng.wait_ge(S[slot_sem(n)], landed[n])


        chunks = []

        def add(kind, r, part, width, blocks, pv, first, last, job_):
            chunks.append(dict(n=len(chunks), kind=kind, r=r, part=part, width=width, blocks=blocks,
                               pv=pv, first=first, last=last, job=job_))
            return ("C", chunks[-1]["n"])

        steps = []
        for r in range(2):
            steps += [("K", J_WIN + r, j) for j in range(4)]
            steps.append(add("win", r, "new", 8, 1, 128, True, False, None))
            steps.append(add("win", r, 0, 512, 4, 128, False, True, J_WIN + r))
        for r in range(4):
            steps += [("K", J_SLC + r, j) for j in range(4)]
            steps.append(add("slc", r, "new", 8, 1, 64, True, False, None))
            steps.append(add("slc", r, 0, 512, 4, 64, False, False, J_SLC + r))
            steps.append(add("slc", r, 1, 512, 4, 64, False, True, J_SLC + r))
        for b in range(8):
            steps.append(add("mla", b, "new", 8, 1, 256, True, False, None))
            for i in range(4):
                steps.append(add("mla", b, i, 256, 2, 256, False, i == 3, J_MLA + 4 * b + i))
        UNITS = 96
        FIRST_STEP = 2
        dt_use, use_of = [], {}
        prev = None
        for st in steps:
            if prev is not None and prev[0] == "C":
                use_of[("T", prev[1])] = len(dt_use)
                dt_use.append("V" if prev[1] % 2 else "A")
            if st[0] == "K":
                use_of[st] = len(dt_use)
                dt_use.append("V" if st[2] % 2 else "A")
            prev = st
        use_of[("T", prev[1])] = len(dt_use)
        dt_use.append("V" if prev[1] % 2 else "A")

        def dt_copied(eng, m):
            if m >= 0:
                eng.wait_ge(S["dt_by_" + dt_use[m]], sum(1 for e in dt_use[:m + 1] if e == dt_use[m]))

        last_chunk = {c["job"]: c["n"] for c in chunks if c["job"] is not None}
        ztiles = []
        for n in (J_GA, J_GB):
            ztiles += [("silu", n, tl, 0) for tl in range(5)]
        ztiles += [("oT", None, kc, 0) for kc in range(8)] + [("oTd", None, 0, 0)]
        for half in range(2):
            for what in range(2):
                ztiles += [("sig", J_GATE + 3 * half + what, tl, half) for tl in range(5)]
            ztiles += [(ab, J_GATE + 3 * half + 2, tl, half) for tl in range(5) for ab in ("pa", "pb")]
        ztiles += [("hT", None, kc, 0) for kc in range(8)] + [("hTd", None, 0, 0)]
        ztiles += [("wo", J_WO + g, tl, g) for tl in range(5) for g in range(2)]
        last_z = {z[1]: v for v, z in enumerate(ztiles) if z[1] is not None}

        def z_by(v):
            kind = ztiles[v][0]
            if kind == "sig":
                return "act"
            if kind in ("oT", "hT"):
                return "act" if ztiles[v][2] % 2 else "dve"
            return "dve"

        def z_free(eng, v):
            if v >= 0:
                eng.wait_ge(S["z_by_" + z_by(v)], sum(1 for x in range(v + 1) if z_by(x) == z_by(v)))

        def slot_free(eng, n):
            m = n - RING
            if 0 <= m < J_WIN:
                eng.wait_ge(S["jobs_used"], m + 1 if m < J_W1 else J_WIN)
            elif J_WIN <= m < J_GA:
                eng.wait_ge(S["do_ps"], last_chunk[m] + 1)
            elif m >= J_GA:
                eng.wait_ge(S["z_ps"], last_z[m] + 1)

        def unit(u):
            s_, t_ = divmod(u, TILES)
            return s_ // 8, s_ % 8, t_

        def pt_by(u):
            return "A" if u % 2 else "V"

        block = ctx.enter_context(nc.Block())

        @block.sync
        def _(sp):
            sp.dma_start(pti[0:8, 0:32], t["pt8"]).then_inc(S["pt_in"], 16)
            sp.dma_start(pti[0:4, 32:96], t["pt4"]).then_inc(S["pt_in"], 16)
            sp.dma_start(pti[0:16, 96:128], t["pt16"]).then_inc(S["pt_in"], 16)
            sp.dma_start(pti[0:1, 128:384], t["ptflat"]).then_inc(S["pt_in"], 16)
            sp.dma_start(cst[:, :], t["const"][:, 0:NC_CST]).then_inc(S["cst_in"], 16)
            sp.dma_start(normpre, t["norm_pre"]).then_inc(S["x_in"], 16)
            sp.dma_start(XG[:, :], t["xT"]).then_inc(S["x_in"], 16)
            for half in range(2):
                for k in range(KM):
                    w = W[:, k * W_ATTN + half * 2 * GW:k * W_ATTN + (half + 1) * 2 * GW]
                    sp.dma_start(w, t["w_attn"][:, k, half * 2 * GW:(half + 1) * 2 * GW]).then_inc(S[f"w_in{half}{k // 2}"], 16)
            sp.dma_start(qnorm, t["q_norm"]).then_inc(S["vec_in"], 16)
            sp.dma_start(kvn, t["kv_norm"].broadcast_to([P, 256])).then_inc(S["vec_in"], 16)
            sp.dma_start(t["o_win"][:, 0:WINDOW - 1, :], t["win"][:, 1:WINDOW, :]).then_inc(S["win_moved"], 16)
            slot_free(sp, J_W1)
            sp.dma_start(job(J_W1)[:, 0:3072], t["w_qup"]).then_inc(S[slot_sem(J_W1)], 16)
            sp.dma_start(job(J_W1)[:, 3072:4096], t["w_k"]).then_inc(S[slot_sem(J_W1)], 16)
            slot_free(sp, J_W2)
            sp.dma_start(job(J_W2)[:, 0:1024], t["w_v"]).then_inc(S[slot_sem(J_W2)], 16)
            sp.dma_start(job(J_W2)[0:64, 1024:3072], t["w_kT"]).then_inc(S[slot_sem(J_W2)], 16)
            sp.dma_start(job(J_W2)[:, 3072:3072 + TOK], t["const"][:, NC_CST:NC_CST + TOK]).then_inc(S[slot_sem(J_W2)], 16)
            for r in range(2):
                n = J_WIN + r
                slot_free(sp, n)
                for j in range(4):
                    dst = job(n)[:, j * 1024:(j + 1) * 1024].rearrange("p (r c) -> p r c", r=4)
                    sp.dma_start(dst, t["win"][4 * r + j].rearrange("(r p) c -> p r c", p=P)).then_inc(S[slot_sem(n)], 16)
            for n in range(J_MLA, J_GA):
                slot_free(sp, n)
                with sp.Fori(0, 8) as q:
                    page = sp.value_load(pti[0:1, bass.ds(q + (128 + (n - J_MLA) * 8), 1)], min_val=0, max_val=319)
                    dst = ring[:, bass.ds(q * 512 + (n % RING) * JOB, 512)]
                    sp.dma_start(dst, t["latent"][bass.ds(page, 1)].rearrange("a p n -> (a p) n")).then_inc(S[slot_sem(n)], 16)
                if n == J_MLA + 2:
                    sp.wait_ge(S["xg_dead"], 1)
                    sp.dma_start(XG[:, :], t["xT"]).then_inc(S["x2_in"], 16)
            def weights(n, src, lo=0, hi=JOB):
                sp.dma_start(job(n)[:, lo:hi], src).then_inc(S[slot_sem(n)], 16)

            for n in range(J_GA, N_JOBS):
                slot_free(sp, n)
                if n < J_GATE:
                    weights(n, t["w_gate"][:, n - J_GA])
                elif n < J_WO:
                    half, what = divmod(n - J_GATE, 3)
                    if what < 2:
                        weights(n, t["w_gate"][:, 2 + 2 * what + half])
                    else:
                        weights(n, t["w_pa"][:, half], 0, 2048)
                        weights(n, t["w_pb"][:, half], 2048, 4096)
                else:
                    weights(n, t["w_out"][:, n - J_WO])
                if n == J_GA:
                    sp.wait_ge(S["do_ps"], len(chunks))
                    sp.dma_start(QZs, t["w_v"]).then_inc(S["wv2_in"], 16)
            slot_free(sp, N_JOBS)
            sp.dma_start(job(N_JOBS).rearrange("p (t c) -> p t c", t=TILES), t["x"][0:SEQ].rearrange("(t p) c -> p t c", p=P)).then_inc(S["xend_in"], 16)
            sp.wait_ge(S["z_ps"], 19)
            z_free(sp, 17)
            z_free(sp, 18)
            sp.dma_start(OA[0:DEC, 0:D_MODEL], t["x"][SEQ:TOK]).then_inc(S["xend_in"], 16)
            sp.dma_start(OB[:, 0:D_MODEL], t["norm_post"].broadcast_to([P, D_MODEL])).then_inc(S["xend_in"], 16)
            for tl in range(5):
                sp.wait_ge(S["y"], tl + 1)
                if tl < TILES:
                    sp.dma_start(t["o_y"][tl * P:(tl + 1) * P], H[:, tl * D_MODEL:(tl + 1) * D_MODEL]).then_inc(S["y_out"], 16)
                else:
                    sp.dma_start(t["o_y"][SEQ:TOK], H[0:DEC, tl * D_MODEL:(tl + 1) * D_MODEL]).then_inc(S["y_out"], 16)
            sp.wait_ge(S["y_out"], 80)
            sp.wait_ge(S["stored"], N_STORED)
            sp.wait_ge(S["win_moved"], 16)

        @block.gpsimd
        def _(pool):
            pool.dma_start(xtok.rearrange("p (t c) -> p t c", t=TILES), t["x"][0:SEQ].rearrange("(t p) c -> p t c", p=P)).then_inc(S["xtok_in"], 16)
            pool.dma_start(xdec[0:DEC], t["x"][SEQ:TOK]).then_inc(S["xtok_in"], 16)
            pool.wait_ge(S["pe_zero"], 1)
            pool.dma_start(petile[0:CMP_BLOCK], t["pe"]).then_inc(S["pe_in"], 16)

            def gather(dst, src, col, sem):
                pool.indirect_dma_start(out=dst, out_offset=None, in_=src,
                                        in_offset=bass.IndirectOffsetOnAxis(ap=idxi[:, col:col + 1], axis=0)).then_inc(sem, 16)

            pool.wait_ge(S["idx"], 2)
            for n in range(J_W1):
                slot_free(pool, n)
                for i in range(2):
                    gather(job(n)[:, i * 2048:(i + 1) * 2048], t["cmp"], 2 * n + i, S[slot_sem(n)])
            pool.wait_ge(S["rot"], 4)
            pool.dma_start(t["o_kv"][0:SEQ].rearrange("(t p) c -> p t c", p=P), pP[:, :, C_KS:C_GN]).then_inc(S["stored"], 16)
            pool.dma_start(t["o_kv"][SEQ:TOK], projD[0:DEC, C_KS:C_GN]).then_inc(S["stored"], 16)
            pool.dma_start(t["o_win"][:, WINDOW - 1, 0:P], projD[0:DEC, C_KW:C_KW + P]).then_inc(S["stored"], 16)
            pool.dma_start(t["o_win"][:, WINDOW - 1, P:2 * P], projD[0:DEC, C_VW:C_VW + P]).then_inc(S["stored"], 16)
            pool.dma_start(t["o_kr"][0:SEQ].rearrange("(t p) c -> p t c", p=P), pP[:, :, C_KR:W_ATTN]).then_inc(S["stored"], 16)
            pool.dma_start(t["o_kr"][SEQ:TOK], projD[0:DEC, C_KR:W_ATTN]).then_inc(S["stored"], 16)
            pool.wait_ge(S["cn"], 1)
            pool.dma_start(t["o_c"][0:SEQ].rearrange("(t p) c -> p t c", p=P), pP[:, :, C_CD:C_KR]).then_inc(S["stored"], 16)
            pool.dma_start(t["o_c"][SEQ:TOK], projD[0:DEC, C_CD:C_KR]).then_inc(S["stored"], 16)
            pool.wait_ge(S["stored"], N_STORED)
            pool.engine_nop().then_inc(S["kv_stored"], 1)
            pool.wait_ge(S["idxs"], 1)
            for r in range(4):
                n = J_SLC + r
                slot_free(pool, n)
                for j in range(4):
                    gather(job(n)[:, j * 1024:(j + 1) * 1024], t["slc"], 96 + 4 * r + j, S[slot_sem(n)])
            for n in range(32):
                if n >= RING:
                    pool.wait_ge(S["do_ps"], last_chunk[J_MLA + n - RING] + 1)
                for i in range(2):
                    gather(KRR[:, (n % RING) * 256 + i * P:(n % RING) * 256 + (i + 1) * P], t["krT"], 32 + 2 * n + i, S[f"kr{n % RING}_landed"])

        GROUPS = [(C_Q + P * k, P) for k in range(4)] * 2 + [(C_KS, P), (C_KW, P)] \
            + [(C_QD + P * j, P) for j in range(3)] + [(C_CD + P * j, P) for j in range(2)] + [(C_KR, ROPE_D)]

        def group_copied(eng, n):
            eng.wait_ge(S["group_by_act" if n % 2 == 0 else "group_by_dve"], n // 2 + 1)

        def K_of(c):
            r, part = c["r"], c["part"]
            out = []
            for j in range(4):
                if c["kind"] == "win":
                    q = QZw[:, (4 * r + j) * 32:(4 * r + j + 1) * 32]
                    out.append([(q, KnW if part == "new" else KTs[:, j * 512:(j + 1) * 512], 0, c["width"])])
                elif c["kind"] == "slc":
                    s2 = 0 if part == "new" else part
                    q = QZs[:, ((4 * r + j) * 2 + s2) * 32:((4 * r + j) * 2 + s2 + 1) * 32]
                    out.append([(q, KnS[:, (j % 2) * 8:(j % 2) * 8 + 8] if part == "new" else KTs[:, j * 512:(j + 1) * 512], 0, c["width"])])
                else:
                    ql = [QL[:, (ck * 8 + r) * 32:(ck * 8 + r + 1) * 32] for ck in range(2)]
                    qr = [QR[:, (r * 4 + v) * 32:(r * 4 + v + 1) * 32] for v in range(4)]
                    if part == "new":
                        out.append([(ql[0], cTn[:, 0:8], 0, 8), (ql[1], cTn[:, 8:16], 0, 8), (qr[0], krn, 0, 8)])
                    else:
                        pages = job(c["job"]).rearrange("p (q c) -> p q c", q=8)
                        kr = KRR[:, ((c["job"] - J_MLA) % RING) * 256:][:, 0:256]
                        row = [(ql[ck], pages[:, 2 * j:2 * j + 2, 256 + ck * P:256 + (ck + 1) * P], 0, 256) for ck in range(2)]
                        for q2 in range(2):
                            q = 2 * j + q2
                            row.append((qr[q % 4], kr[:, (q // 4) * P:(q // 4 + 1) * P], q2 * P, P))
                        out.append(row)
            return out

        def V_of(c, blk, j):
            r, part = c["r"], c["part"]
            if c["kind"] == "win":
                if part == "new":
                    return projD[0:DEC, C_VW:C_VW + P]
                return job(c["job"])[:, j * 1024 + blk * 256 + P:j * 1024 + blk * 256 + 256]
            if c["kind"] == "slc":
                if part == "new":
                    return projD[0:DEC, C_VS + (j % 2) * 64:C_VS + (j % 2) * 64 + 64]
                at = j * 1024 + 512 + (2 * blk + part) * 64
                return job(c["job"])[:, at:at + 64]
            if part == "new":
                return projD[0:DEC, C_CD:C_CD + 256]
            return job(c["job"])[:, (2 * j + blk) * 512:(2 * j + blk) * 512 + 256]

        @block.tensor
        def _(pe):
            ident = C("ident")

            pe.wait_ge(S["cst_in"], 16)
            pe.wait_ge(S["ptf"], 3)
            pe.matmul(bank[7][:, 0:32], C("exp8", rows=8), ptf[0:8, 0:32], start=True, stop=True)
            pe.matmul(bank[7][:, 32:96], C("exp4", rows=4), ptf[0:4, 32:96], start=True, stop=True).then_inc(S["idx_ps"], 1)
            pe.wait_ge(S["pe_in"], 16)
            pe.matmul(bank[6][:, 0:256], C("onesmean"), petile, start=True, stop=True).then_inc(S["mpe_ps"], 1)

            def key_transpose(b):
                pe.wait_ge(S["ctmp"], b + 1)
                if b == 0:
                    pe.wait_ge(S["idx"], 2)
                if b >= 1:
                    pe.wait_ge(S["kct"], b)
                pe.transpose(bank[7][:, 0:P], ctmp[:, (b % 2) * P:(b % 2) * P + P], ident).then_inc(S["kct_ps"], 1)

            for u in range(8):
                half, tl = divmod(u, 4)
                if u >= 2:
                    pe.wait_ge(S["p1_act"], u - 1)
                    pe.wait_ge(S["p1_dve"], u - 1)
                for k in range(KM):
                    if u == 0:
                        pe.wait_ge(S["xg"], k + 1)
                    if tl == 0 and k % 2 == 0:
                        pe.wait_ge(S[f"w_in{half}{k // 2}"], 32)
                    for n in range(2):
                        w = k * W_ATTN + (2 * half + n) * GW
                        mm = pe.matmul(bank[2 * (u % 2) + n][:, 0:GW], XG[:, k * TOK + tl * P:k * TOK + (tl + 1) * P],
                                       W[:, w:w + GW], start=(k == 0), stop=(k == KM - 1))
                mm.then_inc(S["p1"], 1)
                if u >= 1:
                    key_transpose(u - 1)
                b = u
                job_landed(pe, 2 * b)
                job_landed(pe, 2 * b + 1)
                if b == 1:
                    pe.wait_ge(S["mpe"], 1)
                if b >= 2:
                    pe.wait_ge(S["vcd"], b - 1)
                for r in range(8):
                    for i in range(4):
                        src = job(2 * b + i // 2)[:, (i % 2) * 2048 + r * 256:(i % 2) * 2048 + (r + 1) * 256]
                        mm = pe.matmul(bank[5 + b % 2][32 * i:32 * i + 32, 0:256], C("pool"), src,
                                       start=(r == 0), stop=(r == 7))
                mm.then_inc(S["jobs_used"], 2)
            for k in range(KM):
                for n in range(NG):
                    w = k * W_ATTN + n * GW
                    mm = pe.matmul(bank[4][32 * n:32 * n + DEC, 0:GW], XG[:, k * TOK + SEQ:(k + 1) * TOK], W[:, w:w + GW],
                                   start=(k == 0), stop=(k == KM - 1))
            mm.then_inc(S["p1d"], 1)
            key_transpose(7)

            def group(n):
                c, w = GROUPS[n]
                if n < 4:
                    pe.wait_ge(S["p1_act"], 8)
                    pe.wait_ge(S["p1_dve"], 8)
                else:
                    group_copied(pe, n - 4)
                if n == 4:
                    pe.wait_ge(S["rot"], 4)
                if n == 10:
                    pe.wait_ge(S["qdn"], 1)
                if n == 13:
                    pe.wait_ge(S["cn"], 1)
                for tl in range(TILES):
                    mm = pe.transpose(bank[n % 4][0:w, tl * P:(tl + 1) * P], pP[:, tl, c:c + w], ident)
                mm.then_inc(S["group"], 1)

            def group_dec(ns):
                for n in ns:
                    c, w = GROUPS[n]
                    mm = pe.transpose(bank[7][0:w, P + 8 * n:P + 8 * n + 8], projD[0:DEC, c:c + w], C("ident", 0, 8, rows=8))
                mm.then_inc(S["group_dec"], 1)

            pe.wait_ge(S["projd"], 1)
            pe.wait_ge(S["kct"], 8)
            group_dec(range(4))
            for n in range(4):
                group(n)
            pe.wait_ge(S["qzraw"], 8)
            pe.wait_ge(S["vcd"], 8)
            for b in range(8):
                mm = pe.matmul(bank[5][0:64, 0:P], QZraw[:, b * 64:(b + 1) * 64], KcT[:, b * P:(b + 1) * P],
                               start=(b == 0), stop=(b == 7))
            mm.then_inc(S["scd_ps"], 1)
            pe.wait_ge(S["gsig"], 2)
            pe.matmul(bank[6][0:64, 0:24], C("b2bh", rows=8), gsig[0:DEC, 96:120], start=True, stop=True).then_inc(S["gbh_ps"], 1)
            for n in range(4, 10):
                group(n)
            group_dec(range(4, 10))
            for n in range(10, 13):
                group(n)
            for n in range(13, 16):
                group(n)
            group_dec(range(10, 16))

            pe.wait_ge(S["pcd"], 1)
            pe.matmul(bank[5][0:16, P:2 * P], C("headsum", rows=64), pcD[0:64, :], start=True, stop=True)
            pe.transpose(bank[5][:, 256:320], pcD[0:64, :], C("ident", 0, 64, rows=64)).then_inc(S["pcd_ps"], 1)

            pe.wait_ge(S["p1d_out"], 1)
            for tl in range(TILES):
                pe.matmul(bank[4][:, 0:16], pP[:, tl, C_KC:C_KC + P], C("poolp", tl * 16, 16), start=(tl == 0), stop=False)
            pe.matmul(bank[4][:, 0:16], petile[:, 0:P], C("onesmean", 0, 16), start=False, stop=True).then_inc(S["kcp_ps"], 1)
            group_copied(pe, 12)
            for tl in range(TILES):
                pe.matmul(bank[0][0:16, 0:P], C("poolp", tl * 16, 16), pP[:, tl, C_VC:C_VC + P], start=(tl == 0), stop=False)
            pe.matmul(bank[0][0:16, 0:P], C("onesmean", 0, 16), petile[:, P:256], start=False, stop=True).then_inc(S["vcp_ps"], 1)
            pe.wait_ge(S["vcs"], 1)
            group_copied(pe, 13)
            pe.matmul(bank[1][:, 0:P], C("rep16", rows=16), vcs[0:16, :], start=True, stop=True).then_inc(S["vrep_ps"], 1)
            pe.wait_ge(S["kcbd"], 1)
            group_copied(pe, 14)
            for tl in range(TILES):
                for k in range(4):
                    mm = pe.matmul(bank[2][:, tl * P + k * 32:tl * P + (k + 1) * 32], qTraw[:, k * 512 + tl * P:k * 512 + (tl + 1) * P],
                                   kcBD[:, (k // 2) * 32:(k // 2 + 1) * 32], start=True, stop=True)
            mm.then_inc(S["scp_ps"], 1)

            job_landed(pe, J_W1)
            wq, wk = job(J_W1)[:, 0:3072], job(J_W1)[:, 3072:4096]
            qbank = [3, 0, 1, 4]
            group_copied(pe, 15)
            for h in range(8):
                if h == 1:
                    pe.wait_ge(S["vcs"], 1)
                if h == 2:
                    pe.wait_ge(S["vcbd"], 1)
                if h == 3:
                    pe.wait_ge(S["kcbd"], 1)
                if h >= 4:
                    pe.wait_ge(S["qm_act"], h - 3)
                    pe.wait_ge(S["qm_dve"], h - 3)
                for j in range(3):
                    mm = pe.matmul(bank[qbank[h % 4]][:, :], wq[:, j * 1024 + h * P:j * 1024 + (h + 1) * P],
                                   qdnT[:, j * TOK:j * TOK + SEQ], start=(j == 0), stop=(j == 2))
                mm.then_inc(S["qm_ps"], 1)
            pe.wait_ge(S["g3"], 1)
            pe.wait_ge(S["tdec_rest"], 1)
            for h in range(8):
                for j in range(3):
                    mm = pe.matmul(bank[6][:, 64 + 8 * h:72 + 8 * h], wq[:, j * 1024 + h * P:j * 1024 + (h + 1) * P],
                                   qdnT[:, j * TOK + SEQ:(j + 1) * TOK], start=(j == 0), stop=(j == 2))
            mm.then_inc(S["qmd_ps"], 1)
            kbank = [2, 3, 0, 1]
            pe.wait_ge(S["sc_read"], 1)
            pe.wait_ge(S["qm_act"], 8)
            pe.wait_ge(S["qm_dve"], 8)
            for p2 in range(4):
                for ck in range(2):
                    mm = pe.matmul(bank[kbank[p2]][:, :], wk[:, ck * 512 + p2 * P:ck * 512 + (p2 + 1) * P],
                                   cT[:, ck * TOK:ck * TOK + SEQ], start=(ck == 0), stop=(ck == 1))
                mm.then_inc(S["km_ps"], 1)
            job_landed(pe, J_W2)
            wv, wkT = job(J_W2)[:, 0:1024], job(J_W2)[:, 1024:3072]
            vbank = [4, 2, 3, 0]
            for tl in range(TILES):
                if tl:
                    pe.wait_ge(S["km"], tl)
                for ck in range(2):
                    mm = pe.matmul(bank[vbank[tl]][:, :], cT[:, ck * TOK + tl * P:ck * TOK + (tl + 1) * P],
                                   wv[:, ck * 512:(ck + 1) * 512], start=(ck == 0), stop=(ck == 1))
                mm.then_inc(S["vm_ps"], 1)
            pe.wait_ge(S["qmd"], 2)
            pe.wait_ge(S["pcz"], 1)
            for h in range(8):
                for ck in range(2):
                    mm = pe.matmul(bank[6][:, P + ck * 64 + h * 8:P + ck * 64 + h * 8 + 8],
                                   wkT[0:64, h * 256 + ck * P:h * 256 + (ck + 1) * P], qmd[0:64, h * 8:h * 8 + 8],
                                   start=True, stop=True)
            mm.then_inc(S["jobs_used"], 2)
            pe.wait_ge(S["r16"], 1)
            pe.transpose(bank[5][0:16, 0:16], R16[0:16, :], C("ident", 0, 16, rows=16)).then_inc(S["r16T_ps"], 1)
            pe.wait_ge(S["rt16"], 1)
            pe.matmul(bank[5][:, 16:32], C("exp16", rows=16), RT16[0:16, :], start=True, stop=True).then_inc(S["idxs_ps"], 1)
            pe.wait_ge(S["pcp"], 1)
            pe.wait_ge(S["km"], 4)
            for tl in range(TILES):
                mm = pe.transpose(bank[1][:, tl * P:(tl + 1) * P], pcP[:, tl * P:(tl + 1) * P], ident)
            mm.then_inc(S["pcpT_ps"], 1)
            pe.wait_ge(S["idxs"], 1)
            for b in range(8):
                mm = pe.matmul(bank[5][0:64, 384:512], PcZ[:, b * 64:(b + 1) * 64], VcD[:, b * P:(b + 1) * P],
                               start=(b == 0), stop=(b == 7))
            mm.then_inc(S["ocd_ps"], 1)
            pe.wait_ge(S["vm"], 4)
            pe.wait_ge(S["pcpT"], 1)
            for tl in range(TILES):
                pe.matmul(bank[[2, 3, 0, 4][tl]][:, :], Sc[:, tl * P:(tl + 1) * P], VcBD, start=True, stop=True).then_inc(S["ocp_ps"], 1)

            def values(br, tl, kb, h):
                if br < 2:
                    at = kb * 256 + br * P + (h // 4) * 64
                    return VV[:, at:at + 64]
                return vm[:, kb * 512 + h * 64:kb * 512 + (h + 1) * 64]

            def scores(u):
                br, h, tl = unit(u)
                width = (tl + 1) * P
                if u >= 2:
                    pe.wait_ge(S["p"], u - 1)
                if br < 2:
                    e, g = h % 2, h // 4
                    q = qrT[64 * e:64 * e + 64, (h // 2) * 512 + tl * P:(h // 2) * 512 + (tl + 1) * P]
                    kk = KT2[64 * e:64 * e + 64, (br * 2 + g) * 512:(br * 2 + g) * 512 + width]
                else:
                    q = qmT[0:96, h * 512 + tl * P:h * 512 + (tl + 1) * P]
                    kk = kmT[0:96, h * 512:h * 512 + width]
                pe.matmul(bank[u % 2][:, 0:width], q, kk, start=True, stop=False)
                pe.matmul(bank[u % 2][:, tl * P:width], identb[:, :], causb[:, :], start=False, stop=True).then_inc(S["s"], 1)

            def transposes(u):
                _, _, tl = unit(u)
                pe.wait_ge(S["p"], u + 1)
                if u >= 2:
                    pe.wait_ge(S["pt_by_" + pt_by(u - 2)], (u - 2) // 2 + 1)
                for kb in range(tl + 1):
                    mm = pe.transpose(bank[2 + u % 2][:, kb * P:(kb + 1) * P], Pb[u % 3][:, kb * P:(kb + 1) * P], ident)
                mm.then_inc(S["pt_ps"], 1)

            def outputs(u):
                br, h, tl = unit(u)
                pe.wait_ge(S["pt_by_" + pt_by(u)], u // 2 + 1)
                if u >= 1:
                    pe.wait_ge(S["o"], u)
                for kb in range(tl + 1):
                    mm = pe.matmul(bank[4][:, 0:64], PTb[u % 2][:, kb * P:(kb + 1) * P], values(br, tl, kb, h),
                                   start=(kb == 0), stop=(kb == tl))
                mm.then_inc(S["o_ps"], 1)

            def dec_transposes(c):
                dt_copied(pe, use_of[("T", c["n"])] - 1)
                pe.wait_ge(S["dp"], c["n"] + 1)
                w = P if c["part"] != "new" else 8
                for blk in range(c["blocks"]):
                    mm = pe.transpose(bank[6][0:w, blk * P:(blk + 1) * P], Pd[:, blk * P:blk * P + w], ident)
                mm.then_inc(S["dt_ps"], 1)

            def dec_keys(n, j):
                if j == 0:
                    job_landed(pe, n)
                dt_copied(pe, use_of[("K", n, j)] - 1)
                for blk in range(4):
                    if n < J_SLC:
                        src = job(n)[:, j * 1024 + blk * 256:j * 1024 + blk * 256 + P]
                    else:
                        src = job(n)[:, j * 1024 + blk * P:j * 1024 + (blk + 1) * P]
                    mm = pe.transpose(bank[6][:, blk * P:(blk + 1) * P], src, ident)
                mm.then_inc(S["dt_ps"], 1)

            def dec_scores(c):
                if c["n"] >= 1:
                    pe.wait_ge(S["dp"], c["n"])
                if c["kind"] == "mla" and c["part"] != "new":
                    job_landed(pe, c["job"])
                    m = c["job"] - J_MLA
                    pe.wait_ge(S[f"kr{m % RING}_landed"], 32 * (m // RING + 1))
                if c["kind"] != "mla" and c["part"] != "new":
                    for j in (2, 3):
                        dt_copied(pe, use_of[("K", c["job"], j)])
                rows = K_of(c)
                for x in range(len(rows[0])):
                    for j in range(4):
                        q, kk, at, w = rows[j][x]
                        mm = pe.matmul(bank[5][32 * j:32 * j + 32, at:at + w], q, kk,
                                       start=(x == 0), stop=(x == len(rows[0]) - 1))
                mm.then_inc(S["ds"], 1)

            def dec_outputs(c):
                dt_copied(pe, use_of[("T", c["n"])])
                if c["n"] >= 1:
                    pe.wait_ge(S["do"], c["n"])
                k = DEC if c["part"] == "new" else P
                for blk in range(c["blocks"]):
                    for j in range(4):
                        mm = pe.matmul(bank[7][32 * j:32 * j + 32, 0:c["pv"]], PTd[0:k, blk * P + 32 * j:blk * P + 32 * j + 32],
                                       V_of(c, blk, j), start=(blk == 0), stop=(blk == c["blocks"] - 1))
                mm.then_inc(S["do_ps"], 1)

            pe.wait_ge(S["prep_dve"], 1)
            pe.wait_ge(S["prep_act"], 1)
            prev = None
            for u in range(UNITS + 3):
                st = steps[u - FIRST_STEP] if FIRST_STEP <= u < FIRST_STEP + len(steps) else None
                if prev is not None:
                    dec_transposes(prev)
                if u < UNITS:
                    scores(u)
                if st is not None and st[0] == "K":
                    dec_keys(st[1], st[2])
                if st is not None and st[0] == "C":
                    dec_scores(chunks[st[1]])
                if 2 <= u < UNITS + 2:
                    transposes(u - 2)
                if u >= 3:
                    outputs(u - 3)
                if prev is not None:
                    dec_outputs(prev)
                prev = chunks[st[1]] if st is not None and st[0] == "C" else None

            pe.wait_ge(S["mrg"], 1)
            pe.transpose(bank[5][0:8, 0:P], mrg[:, 0:8], ident)
            pe.transpose(bank[5][0:8, P:2 * P], mrg[:, 8:16], ident).then_inc(S["mrg_ps"], 1)
            for r in range(4):
                pe.matmul(bank[7][0:64, 0:64], C("selS", r * 64, 64), owS[:, r * 64:(r + 1) * 64], start=(r == 0), stop=(r == 3))
            for r in range(2):
                mm = pe.matmul(bank[7][0:64, 64:128], C("selW", r * 64, 64), mrg[:, 320 + r * 64:320 + (r + 1) * 64], start=(r == 0), stop=(r == 1))
            mm.then_inc(S["ob_ps"], 1)
            pe.wait_ge(S["oa64"], 1)
            for h in range(8):
                mm = pe.matmul(bank[4][0:DEC, h * 64:(h + 1) * 64], C("selT", h * 8, 8, rows=64), od1[0:64, :], start=True, stop=True)
            mm.then_inc(S["oad_ps"], 1)
            pe.wait_ge(S["coef"], 1)
            pe.transpose(bank[5][:, 256:264], mrg[0:8, 16:16 + P], C("ident", 0, 8, rows=8)).then_inc(S["coef_ps"], 1)
            pe.wait_ge(S["wsel"], 1)
            for b in range(8):
                for ck in range(2):
                    mm = pe.matmul(bank[6][:, ck * 64 + b * 8:ck * 64 + b * 8 + 8], OF[:, b * 256 + ck * P:b * 256 + (ck + 1) * P],
                                   Wsel[:, b * 8:b * 8 + 8], start=True, stop=True)
            mm.then_inc(S["olat_ps"], 1)
            pe.wait_ge(S["olat"], 1)
            pe.wait_ge(S["wv2_in"], 16)
            for h in range(8):
                for ck in range(2):
                    mm = pe.matmul(bank[5][0:DEC, h * 64:(h + 1) * 64], mrg[:, 192 + ck * 64 + h * 8:192 + ck * 64 + h * 8 + 8],
                                   QZs[:, ck * 512 + h * 64:ck * 512 + (h + 1) * 64], start=(ck == 0), stop=(ck == 1))
            mm.then_inc(S["obd_ps"], 1)

            for v, (kind, n, x, half) in enumerate(ztiles):
                bk = bank[v % 4]
                z_free(pe, v - 4)
                if v == 0:
                    pe.wait_ge(S["o"], UNITS)
                    pe.wait_ge(S["xg2"], KM)
                m = P if x < TILES else DEC
                lo = x * P
                if kind in ("silu", "sig"):
                    if x == 0:
                        job_landed(pe, n)
                    for k in range(KM):
                        mm = pe.matmul(bk[0:m, :], XG[:, k * TOK + lo:k * TOK + lo + m], job(n)[:, k * 512:(k + 1) * 512],
                                       start=(k == 0), stop=(k == KM - 1))
                elif kind in ("oT", "hT"):
                    if x == 0:
                        pe.wait_ge(S["gated" if kind == "oT" else "h"], 10)
                    for tl in range(TILES):
                        if kind == "oT":
                            src = (OA if x < 4 else OB)[:, tl * 512 + (x % 4) * P:tl * 512 + (x % 4 + 1) * P]
                        else:
                            src = H[:, tl * D_MODEL + x * P:tl * D_MODEL + (x + 1) * P]
                        mm = pe.transpose(bk[:, tl * P:(tl + 1) * P], src, ident)
                elif kind in ("oTd", "hTd"):
                    for kc in range(8):
                        if kind == "oTd":
                            src = (OA if kc < 4 else OB)[0:DEC, TILES * 512 + (kc % 4) * P:TILES * 512 + (kc % 4 + 1) * P]
                        else:
                            src = H[0:DEC, TILES * D_MODEL + kc * P:TILES * D_MODEL + (kc + 1) * P]
                        mm = pe.transpose(bk[:, kc * 8:kc * 8 + 8], src, C("ident", 0, 8, rows=8))
                elif kind in ("pa", "pb"):
                    ab = 0 if kind == "pa" else 1
                    if x == 0 and ab == 0:
                        job_landed(pe, n)
                        if half == 0:
                            z_free(pe, 16)
                            z_free(pe, 17)
                            z_free(pe, 18)
                    for k in range(4):
                        mm = pe.matmul(bk[0:m, :], oT[:, (4 * ab + k) * TOK + lo:(4 * ab + k) * TOK + lo + m],
                                       job(n)[:, ab * 2048 + k * 512:ab * 2048 + (k + 1) * 512], start=(k == 0), stop=(k == 3))
                else:
                    if x == 0:
                        job_landed(pe, n)
                        if half == 0:
                            for q in (v - 1, v - 2, v - 3):
                                z_free(pe, q)
                    for k in range(KM):
                        mm = pe.matmul(bk[0:m, :], hT[:, k * TOK + lo:k * TOK + lo + m], job(n)[:, k * 512:(k + 1) * 512],
                                       start=(k == 0), stop=(k == KM - 1))
                mm.then_inc(S["z_ps"], 1)

        @block.scalar
        def _(act):
            own = [0]

            def mark(ins):
                own[0] += 1
                ins.then_inc(S["act_own"], 1)

            def settle():
                act.wait_ge(S["act_own"], own[0])

            def copy(dst, src, scale=1.0):
                return act.activation(dst, src, ACT.Copy, scale=scale)

            act.wait_ge(S["ss_init"], 1)
            act.wait_ge(S["xtok_in"], 32)
            for tl in range(5):
                rows = P if tl < TILES else DEC
                src = xtok[:, tl * D_MODEL:(tl + 1) * D_MODEL] if tl < TILES else xdec[0:DEC]
                ins = act.activation(sqs[0:rows], src, ACT.Square, accum_out=ss5[0:rows, tl:tl + 1])
                if tl == 4:
                    ins.then_inc(S["ss"], 1)
                else:
                    mark(ins)
                    settle()
            act.wait_ge(S["v5"], 1)
            act.activation(rt5, v5, ACT.Sqrt).then_inc(S["rt5"], 1)

            def kct(b):
                act.wait_ge(S["kct_ps"], b + 1)
                copy(KcT[:, b * P:(b + 1) * P], bank[7][:, 0:P]).then_inc(S["kct"], 1)

            act.wait_ge(S["rs5"], 1)
            for u in range(8):
                half, tl = divmod(u, 4)
                act.wait_ge(S["p1"], u + 1)
                at = tl * W_ATTN + 2 * half * GW
                act.activation(projP[:, at:at + GW], bank[2 * (u % 2)][:, 0:GW], ACT.Copy, scale=rs5[:, tl:tl + 1]).then_inc(S["p1_act"], 1)
                if u >= 1:
                    kct(u - 1)
            kct(7)
            act.wait_ge(S["p1_act"], 8)
            act.wait_ge(S["p1_dve"], 8)
            act.activation(gsig[:, 0:96].rearrange("p (t c) -> p t c", t=TILES), pP[:, :, C_GN:C_QD], ACT.Sigmoid).then_inc(S["gsig"], 1)
            act.wait_ge(S["projd"], 1)
            act.activation(gsig[0:DEC, 96:120], projD[0:DEC, C_GN:C_QD], ACT.Sigmoid).then_inc(S["gsig"], 1)
            for tl in range(5):
                for x, (c, w) in enumerate(((C_QD, Q_LORA), (C_CD, KV_LORA))):
                    rows = P if tl < TILES else DEC
                    src = pP[:, tl, c:c + w] if tl < TILES else projD[0:DEC, c:c + w]
                    if tl == 0 and x == 0:
                        act.wait_ge(S["group"], 1)
                    ins = act.activation(sq2[0:rows, 0:w], src, ACT.Square, accum_out=ss10[0:rows, 2 * tl + x:2 * tl + x + 1])
                    if tl == 4 and x == 1:
                        ins.then_inc(S["ss10"], 1)
                    else:
                        mark(ins)
                        settle()

            def group(n):
                act.wait_ge(S["group"], n + 1)
                bk = bank[n % 4]
                if n < 4:
                    ins = copy(qTraw[:, n * 512:(n + 1) * 512], bk[:, :], NSA_SCALE)
                elif n < 8:
                    ins = copy(qrT[:, (n - 4) * 512:(n - 3) * 512], bk[:, :], NSA_SCALE)
                elif n == 8:
                    for g in range(2):
                        for e in range(2):
                            ins = copy(KT2[64 * e:64 * e + 64, g * 512:(g + 1) * 512], bk[64 * g:64 * g + 64, :])
                elif n < 13:
                    j = n - 10
                    ins = act.activation(qdnT[:, j * TOK:j * TOK + SEQ], bk[:, :], ACT.Copy, scale=qnorm[:, j:j + 1])
                else:
                    ins = copy(cT[:, (n - 13) * TOK:(n - 13) * TOK + SEQ], bk[:, :])
                ins.then_inc(S["group_by_act"], 1)

            group(0)
            group(2)
            act.wait_ge(S["v10"], 1)
            act.activation(rt10, v10, ACT.Sqrt).then_inc(S["rt10"], 1)
            act.wait_ge(S["nmc"], 1)
            act.activation(pcD[0:64], bank[5][0:64, 0:P], ACT.Exp, bias=nmc[0:64], accum_out=rsc[0:64]).then_inc(S["pce"], 1)
            act.wait_ge(S["vec_in"], 32)
            for n in (4, 6, 8, 10, 12, 14):
                group(n)
            act.wait_ge(S["scs"], 1)
            act.activation(pcP, Sc, ACT.Exp).then_inc(S["pcpe"], 1)
            for h in range(8):
                act.wait_ge(S["qm_ps"], h + 1)
                copy(qmT[0:64, h * 512:(h + 1) * 512], bank[[3, 0, 1, 4][h % 4]][0:64, :], MLA_SCALE).then_inc(S["qm_act"], 1)
            act.wait_ge(S["qmd_ps"], 1)
            copy(qmd[0:64], bank[6][0:64, 64:128], MLA_SCALE).then_inc(S["qmd"], 1)
            for p2 in range(4):
                act.wait_ge(S["km_ps"], p2 + 1)
                bk = bank[[2, 3, 0, 1][p2]]
                copy(kmT[0:64, 2 * p2 * 512:(2 * p2 + 1) * 512], bk[0:64, :])
                copy(kmT[0:64, (2 * p2 + 1) * 512:(2 * p2 + 2) * 512], bk[64:128, :]).then_inc(S["km"], 1)
            for tl in range(TILES):
                act.wait_ge(S["vm_ps"], tl + 1)
                copy(vm[:, tl * 512:(tl + 1) * 512], bank[[4, 2, 3, 0][tl]][:, :]).then_inc(S["vm"], 1)
            act.wait_ge(S["vm"], 4)
            act.nop().then_inc(S["prep_act"], 1)

            def exps(u):
                _, _, tl = unit(u)
                w = (tl + 1) * P
                act.wait_ge(S["nm"], u + 1)
                if u >= 3:
                    act.wait_ge(S["pt_ps"], u - 2)
                act.activation(Pb[u % 3][:, 0:w], bank[u % 2][:, 0:w], ACT.Exp, bias=NMp[:, u:u + 1],
                               accum_out=RSp[:, u:u + 1]).then_inc(S["p"], 1)

            def pt_copy(u):
                _, _, tl = unit(u)
                act.wait_ge(S["pt_ps"], u + 1)
                if u >= 2:
                    act.wait_ge(S["o_ps"], u - 1)
                copy(PTb[u % 2][:, 0:(tl + 1) * P], bank[2 + u % 2][:, 0:(tl + 1) * P]).then_inc(S["pt_by_A"], 1)

            def dec_exp(c):
                n = c["n"]
                act.wait_ge(S["dnm"], n + 1)
                if not c["first"]:
                    act.activation(ALd[:, n:n + 1], NMd[:, n - 1:n], ACT.Exp, bias=NMd[:, n:n + 1], scale=-1.0)
                if n >= 1:
                    act.wait_ge(S["dt_ps"], use_of[("T", n - 1)] + 1)
                act.activation(Pd[:, 0:c["width"]], bank[5][:, 0:c["width"]], ACT.Exp, bias=NMd[:, n:n + 1],
                               accum_out=RSd[:, n:n + 1]).then_inc(S["dp"], 1)

            def dt_copy(st):
                m = use_of[st]
                if dt_use[m] != "A":
                    return
                act.wait_ge(S["dt_ps"], m + 1)
                if st[0] == "K":
                    before = sum(1 for x in steps[:steps.index(st)] if x[0] == "C")
                    if before:
                        act.wait_ge(S["ds"], before)
                    copy(KTs[:, st[2] * 512:(st[2] + 1) * 512], bank[6][:, :]).then_inc(S["dt_by_A"], 1)
                else:
                    c = chunks[st[1]]
                    if c["n"] >= 1:
                        act.wait_ge(S["do_ps"], c["n"])
                    k = DEC if c["part"] == "new" else P
                    copy(PTd[0:k, 0:c["blocks"] * P], bank[6][0:k, 0:c["blocks"] * P]).then_inc(S["dt_by_A"], 1)

            act.wait_ge(S["prep_dve"], 1)
            prev = None
            for u in range(UNITS + 3):
                st = steps[u - FIRST_STEP] if FIRST_STEP <= u < FIRST_STEP + len(steps) else None
                if prev is not None:
                    dt_copy(("T", prev["n"]))
                if u < UNITS:
                    exps(u)
                if st is not None and st[0] == "K":
                    dt_copy(st)
                if st is not None and st[0] == "C":
                    dec_exp(chunks[st[1]])
                if 2 <= u < UNITS + 2 and pt_by(u - 2) == "A":
                    pt_copy(u - 2)
                prev = chunks[st[1]] if st is not None and st[0] == "C" else None

            act.wait_ge(S["mrg_d"], 1)
            act.activation(Pd[0:8, P:2 * P], Pd[0:8, 0:P], ACT.Exp).then_inc(S["mrg_e"], 1)

            n_sg = 0
            for v, (kind, n, x, half) in enumerate(ztiles):
                m = P if x < TILES else DEC
                bk = bank[v % 4]
                if kind == "silu":
                    act.wait_ge(S["z_ps"], v + 1)
                    if n_sg >= 2:
                        act.wait_ge(S["gated"], n_sg - 1)
                    if n_sg == 0:
                        act.wait_ge(S["o"], UNITS)
                    act.activation(sA[0:m, (n_sg % 2) * 512:(n_sg % 2 + 1) * 512], bk[0:m, :], ACT.Sigmoid, scale=rs5[0:m, x:x + 1]).then_inc(S["sg"], 1)
                    n_sg += 1
                elif kind == "sig":
                    act.wait_ge(S["z_ps"], v + 1)
                    if half == 0:
                        act.wait_ge(S["gated"], 10)
                    else:
                        act.wait_ge(S["h"], 5)
                    dst = sA if (n - J_GATE) % 3 == 0 else sB
                    act.activation(dst[0:m, x * 512:(x + 1) * 512], bk[0:m, :], ACT.Sigmoid, scale=rs5[0:m, x:x + 1]).then_inc(S["z_by_act"], 1)
                elif kind in ("oT", "hT") and z_by(v) == "act":
                    act.wait_ge(S["z_ps"], v + 1)
                    copy((oT if kind == "oT" else hT)[:, x * TOK:x * TOK + SEQ], bk[:, :]).then_inc(S["z_by_act"], 1)
                elif kind == "wo":
                    act.wait_ge(S["zc"], 2 * x + half + 1)
                    if x or half:
                        act.wait_ge(S["sqz"], 2 * x + half)
                    at = x * D_MODEL + half * 512
                    act.activation(sA[0:m, 0:512], H[0:m, at:at + 512], ACT.Square, accum_out=ssz[0:m, 2 * x + half:2 * x + half + 1]).then_inc(S["sqz"], 1)
            act.wait_ge(S["vz"], 1)
            act.activation(rtz, vz, ACT.Sqrt).then_inc(S["rtz"], 1)

        @block.vector
        def _(dve):
            own = [0]

            def mark(ins):
                own[0] += 1
                ins.then_inc(S["dve_own"], 1)

            def settle():
                dve.wait_ge(S["dve_own"], own[0])

            def ts(dst, src, a, op, b=None, op1=None):
                if b is None:
                    return dve.tensor_scalar(dst, src, a, None, op)
                return dve.tensor_scalar(dst, src, a, b, op, op1)

            def root_inverse(r, v, rt, tmp, done):
                mark(dve.reciprocal(r, rt))
                settle()
                mark(dve.tensor_tensor(tmp, r, r, ALU.mult))
                settle()
                mark(dve.tensor_tensor(tmp, tmp, v, ALU.mult))
                settle()
                mark(ts(tmp, tmp, -0.5, ALU.mult, 1.5, ALU.add))
                settle()
                dve.tensor_tensor(r, r, tmp, ALU.mult).then_inc(done, 1)
                dve.wait_ge(done, 1)

            dve.memset(petile, 0.0).then_inc(S["pe_zero"], 1)
            mark(dve.memset(ss10, 1.0))
            mark(dve.memset(ssz, 1.0))
            dve.memset(ss5, 1.0).then_inc(S["ss_init"], 1)
            mark(dve.memset(QZraw, 0.0))
            mark(dve.memset(PcZ, 0.0))
            mark(dve.memset(KnS, 0.0))
            mark(dve.memset(krn, 0.0))
            dve.wait_ge(S["pt_in"], 64)
            dve.tensor_copy(ptf[0:8, 0:32], pti[0:8, 0:32]).then_inc(S["ptf"], 1)
            dve.tensor_copy(ptf[0:4, 32:96], pti[0:4, 32:96]).then_inc(S["ptf"], 1)
            dve.tensor_copy(ptf[0:16, 96:128], pti[0:16, 96:128]).then_inc(S["ptf"], 1)
            dve.wait_ge(S["cst_in"], 16)
            mark(dve.tensor_copy(identb[:, :], C("ident")))
            mark(dve.tensor_copy(causb[:, :], C("causal")))
            dve.wait_ge(S["idx_ps"], 1)
            ts(idxi[:, 0:32], bank[7][:, 0:32], 16.0, ALU.mult, C("mod", 0, 1), ALU.add).then_inc(S["idx"], 1)
            ts(idxi[:, 32:96], bank[7][:, 32:96], 32.0, ALU.mult, C("mod", 1, 1), ALU.add).then_inc(S["idx"], 1)
            dve.wait_ge(S["x_in"], 32)
            for k in range(KM):
                ts(XG[:, k * TOK:(k + 1) * TOK], XG[:, k * TOK:(k + 1) * TOK], normpre[:, k:k + 1], ALU.mult).then_inc(S["xg"], 1)
            dve.wait_ge(S["mpe_ps"], 1)
            dve.tensor_copy(mpe, bank[6][:, 0:256]).then_inc(S["mpe"], 1)
            dve.wait_ge(S["ss"], 1)
            ts(v5, ss5, 1.0 / D_MODEL, ALU.mult, EPS, ALU.add).then_inc(S["v5"], 1)
            dve.wait_ge(S["v5"], 1)
            dve.wait_ge(S["rt5"], 1)
            root_inverse(rs5, v5, rt5, tcol[:, 0:5], S["rs5"])
            dve.wait_ge(S["mpe"], 1)
            for u in range(8):
                half, tl = divmod(u, 4)
                dve.wait_ge(S["p1"], u + 1)
                at = tl * W_ATTN + (2 * half + 1) * GW
                ts(projP[:, at:at + GW], bank[2 * (u % 2) + 1][:, 0:GW], rs5[:, tl:tl + 1], ALU.mult).then_inc(S["p1_dve"], 1)
                dve.wait_ge(S["jobs_used"], 2 * (u + 1))
                if u >= 2:
                    dve.wait_ge(S["kct_ps"], u - 1)
                bk = bank[5 + u % 2]
                dve.tensor_tensor(ctmp[:, (u % 2) * P:(u % 2 + 1) * P], bk[:, 0:P], mpe[:, 0:P], ALU.add).then_inc(S["ctmp"], 1)
                dve.tensor_tensor(VcD[:, u * P:(u + 1) * P], bk[:, P:256], mpe[:, P:256], ALU.add).then_inc(S["vcd"], 1)
            dve.wait_ge(S["p1d"], 1)
            for n in range(NG):
                ins = dve.tensor_copy(projD[0:DEC, n * GW:(n + 1) * GW], bank[4][32 * n:32 * n + DEC, 0:GW])
                if n < NG - 1:
                    mark(ins)
                else:
                    ins.then_inc(S["p1d_out"], 1)
            settle()
            dve.wait_ge(S["p1d_out"], 1)
            ts(projD[0:DEC, :], projD[0:DEC, :], rs5[0:DEC, 4:5], ALU.mult).then_inc(S["projd"], 1)
            mark(dve.memset(QZw, 0.0))
            mark(dve.memset(QL, 0.0))
            settle()
            dve.wait_ge(S["group_dec"], 1)
            qz = QZraw.rearrange("p (b c) -> p b c", b=8)
            for h in range(8):
                e, g, k = h % 2, h // 4, h // 2
                dst = QZraw[64 * g:64 * g + 64, h:h + 7 * 72 + 1:72]
                ts(dst, bank[7][64 * e:64 * e + 64, P + 8 * k:P + 8 * k + 8], NSA_SCALE, ALU.mult).then_inc(S["qzraw"], 1)

            def group(n):
                dve.wait_ge(S["group"], n + 1)
                bk = bank[n % 4]
                if n < 4:
                    ins = ts(qTraw[:, n * 512:(n + 1) * 512], bk[:, :], NSA_SCALE, ALU.mult)
                elif n < 8:
                    ins = ts(qrT[:, (n - 4) * 512:(n - 3) * 512], bk[:, :], NSA_SCALE, ALU.mult)
                elif n == 9:
                    for g in range(2):
                        for e in range(2):
                            ins = dve.tensor_copy(KT2[64 * e:64 * e + 64, (2 + g) * 512:(3 + g) * 512], bk[64 * g:64 * g + 64, :])
                elif n == 11:
                    ins = ts(qdnT[:, TOK:TOK + SEQ], bk[:, :], qnorm[:, 1:2], ALU.mult)
                elif n == 13:
                    ins = dve.tensor_copy(cT[:, 0:SEQ], bk[:, :])
                else:
                    ins = dve.tensor_copy(kmT[64:96, 0:SEQ], bk[0:32, :])
                ins.then_inc(S["group_by_dve"], 1)

            group(1)
            group(3)
            dve.wait_ge(S["scd_ps"], 1)
            dve.tensor_reduce(nmc[0:64], bank[5][0:64, 0:P], AX_X, ALU.max, negate=True).then_inc(S["nmc"], 1)
            dve.wait_ge(S["gbh_ps"], 1)
            mark(dve.tensor_tensor(bh24[0:64], bank[6][0:64, 0:24], C("own3", rows=64), ALU.mult))
            settle()
            dve.tensor_reduce(g3[0:64], bh24[0:64].rearrange("p (h c) -> p c h", h=8), AX_X, ALU.add).then_inc(S["g3"], 1)

            def rotate(x, half, heads, cos, sin, rows, tiles):
                n = tiles * heads * half

                def v4(ap):
                    return ap[0:rows, 0:n].rearrange("p (t h c) -> p t h c", t=tiles, h=heads)

                def table(tb):
                    return tb.rearrange("p (t c) -> p t c", t=tiles).unsqueeze(2).broadcast_to([rows, tiles, heads, half])

                x1, x2 = x[:, :, :, 0:half], x[:, :, :, half:2 * half]
                prod = [v4(tmpA[:, i * 384:(i + 1) * 384]) for i in range(4)]
                settle()
                mark(dve.tensor_tensor(prod[0], x1, table(cos), ALU.mult))
                mark(dve.tensor_tensor(prod[1], x2, table(sin), ALU.mult))
                mark(dve.tensor_tensor(prod[2], x1, table(sin), ALU.mult))
                mark(dve.tensor_tensor(prod[3], x2, table(cos), ALU.mult))
                settle()
                mark(dve.tensor_tensor(x1, prod[0], prod[1], ALU.subtract))
                dve.tensor_tensor(x2, prod[2], prod[3], ALU.add).then_inc(S["rot"], 1)
                settle()

            dve.wait_ge(S["group"], 4)
            rotate(pP[:, :, 0:768].rearrange("p t (h c) -> p t h c", h=12), 8, 12, C("cos8", 0, 32), C("sin8", 0, 32), P, TILES)
            dve.wait_ge(S["rot"], 1)
            rotate(projD[0:DEC, 0:768].rearrange("p (t h c) -> p t h c", t=1, h=12), 8, 12, C("cos8", 32, 8, rows=8), C("sin8", 32, 8, rows=8), DEC, 1)
            dve.wait_ge(S["rot"], 2)
            rotate(pP[:, :, C_KR:W_ATTN].unsqueeze(2), 16, 1, C("cos16", 0, 64), C("sin16", 0, 64), P, TILES)
            dve.wait_ge(S["rot"], 3)
            rotate(projD[0:DEC, C_KR:W_ATTN].rearrange("p (t h c) -> p t h c", t=1, h=1), 16, 1, C("cos16", 64, 16, rows=8), C("sin16", 64, 16, rows=8), DEC, 1)
            dve.wait_ge(S["ss10"], 1)
            ss2, v2 = ss10.rearrange("p (t c) -> p t c", c=2), v10.rearrange("p (t c) -> p t c", c=2)
            mark(ts(v2[:, :, 0], ss2[:, :, 0], 1.0 / Q_LORA, ALU.mult, EPS, ALU.add))
            ts(v2[:, :, 1], ss2[:, :, 1], 1.0 / KV_LORA, ALU.mult, EPS, ALU.add).then_inc(S["v10"], 1)
            settle()
            dve.wait_ge(S["v10"], 1)
            dve.wait_ge(S["rt10"], 1)
            tmp10 = tmpA[:, 0:10]
            dve.wait_ge(S["rot"], 4)
            root_inverse(rs10, v10, rt10, tmp10, S["rs10"])
            for tl in range(5):
                x = pP[:, tl, C_QD:C_CD] if tl < TILES else projD[0:DEC, C_QD:C_CD]
                ins = ts(x, x, rs10[0:P if tl < TILES else DEC, 2 * tl:2 * tl + 1], ALU.mult)
                if tl == 4:
                    ins.then_inc(S["qdn"], 1)
            dve.wait_ge(S["vec_in"], 32)
            for tl in range(5):
                rows = P if tl < TILES else DEC
                x = pP[:, tl, C_CD:C_KR] if tl < TILES else projD[0:DEC, C_CD:C_KR]
                ins = dve.scalar_tensor_tensor(x, x, rs10[0:rows, 2 * tl + 1:2 * tl + 2], kvn[0:rows], ALU.mult, ALU.mult)
                if tl == 4:
                    ins.then_inc(S["cn"], 1)
            dve.wait_ge(S["pce"], 1)
            mark(dve.reciprocal(rcc[0:64], rsc[0:64]))
            settle()
            ts(pcD[0:64], pcD[0:64], rcc[0:64], ALU.mult).then_inc(S["pcd"], 1)
            group(5)
            group(7)
            group(9)
            mark(dve.tensor_copy(VV[:, :].rearrange("p (t c) -> p t c", t=TILES), pP[:, :, C_VS:C_KC]))
            group(11)
            group(13)
            group(15)
            dve.wait_ge(S["group_dec"], 3)

            def dcol(n, rows=slice(0, P)):
                return bank[7][rows, P + 8 * n:P + 8 * n + 8]

            for g in range(2):
                for e in range(2):
                    dst = QZw.rearrange("p (b c) -> p b c", b=8)[64 * g:64 * g + 64, :, 4 * g + e:4 * g + e + 3:2]
                    src = bank[7][64 * e:64 * e + 64, P + 8 * (4 + 2 * g):P + 8 * (6 + 2 * g)].rearrange("p (k b) -> p b k", k=2)
                    mark(ts(dst, src, NSA_SCALE, ALU.mult))
                mark(dve.tensor_copy(KnS[0:64, 8 * g:8 * g + 8], dcol(8, slice(64 * g, 64 * g + 64))))
            mark(dve.tensor_copy(KnW, dcol(9)))
            for j in range(3):
                mark(ts(qdnT[:, j * TOK + SEQ:(j + 1) * TOK], dcol(10 + j), qnorm[:, j:j + 1], ALU.mult))
            mark(dve.tensor_copy(cTn[:, 0:8], dcol(13)))
            mark(dve.tensor_copy(cTn[:, 8:16], dcol(14)))
            dve.tensor_copy(krn[0:32], dcol(15, slice(0, 32))).then_inc(S["tdec_rest"], 1)
            mark(dve.memset(kcBD, 0.0))
            settle()
            dve.wait_ge(S["kcp_ps"], 1)
            for g in range(2):
                for e in range(2):
                    ins = dve.tensor_copy(kcBD[64 * e:64 * e + 64, g * 32 + e * 16:g * 32 + e * 16 + 16], bank[4][64 * g:64 * g + 64, 0:16])
                    if g + e < 2:
                        mark(ins)
            ins.then_inc(S["kcbd"], 1)
            dve.wait_ge(S["vcp_ps"], 1)
            dve.tensor_copy(vcs[0:16], bank[0][0:16, 0:P]).then_inc(S["vcs"], 1)
            dve.wait_ge(S["vrep_ps"], 1)
            dve.tensor_tensor(VcBD.rearrange("p (g h c) -> p g h c", g=2, h=4),
                              bank[1][:, 0:P].rearrange("p (g c) -> p g c", g=2).unsqueeze(2).broadcast_to([P, 2, 4, 64]),
                              C("headsel16").rearrange("p (g h) -> p g h", g=2).unsqueeze(3).broadcast_to([P, 2, 4, 64]),
                              ALU.mult).then_inc(S["vcbd"], 1)
            dve.wait_ge(S["scp_ps"], 1)

            def by_block(ap, lo=0):
                return ap.rearrange("p (t n) -> p t n", t=TILES).unsqueeze(2).broadcast_to([P, TILES, 8, 16])

            def by_head(ap):
                return ap.unsqueeze(2).broadcast_to([P, 32, 16])

            s4 = Sc.rearrange("p (t h n) -> p t h n", t=TILES, h=8)
            s3 = Sc.rearrange("p (x n) -> p x n", n=16)
            p4 = pcP.rearrange("p (t h n) -> p t h n", t=TILES, h=8)
            p3 = pcP.rearrange("p (x n) -> p x n", n=16)
            dve.tensor_tensor(s4, bank[2][:, :].rearrange("p (t h n) -> p t h n", t=TILES, h=8), by_block(C("cmaskneg")), ALU.add).then_inc(S["sc_read"], 1)
            dve.wait_ge(S["sc_read"], 1)
            mark(dve.tensor_reduce(cs32[:, 0:32], s3, AX_X, ALU.max))
            settle()
            dve.tensor_tensor(s3, s3, by_head(cs32[:, 0:32]), ALU.subtract).then_inc(S["scs"], 1)
            dve.wait_ge(S["pcpe"], 1)
            mark(dve.tensor_reduce(cs32[:, 32:64], p3, AX_X, ALU.add))
            settle()
            mark(dve.reciprocal(cs32[:, 64:96], cs32[:, 32:64]))
            mark(dve.tensor_tensor(p4, p4, by_block(C("cmask01")), ALU.mult))
            settle()
            dve.wait_ge(S["gsig"], 2)
            mark(dve.tensor_tensor(cs32[:, 32:64], cs32[:, 64:96], gsig[:, 0:96].rearrange("p (x c) -> p x c", c=3)[:, :, 0], ALU.mult))
            settle()
            dve.tensor_tensor(p3, p3, by_head(cs32[:, 32:64]), ALU.mult).then_inc(S["pcp"], 1)

            dve.wait_ge(S["pcd_ps"], 1)
            mark(dve.tensor_reduce(impD[0:16], bank[5][0:16, P:2 * P].rearrange("p (n c) -> p n c", c=2), AX_X, ALU.add))
            for b in range(8):
                ins = dve.tensor_copy(PcZ[:, b * 72:b * 72 + 8], bank[5][:, 256 + 8 * b:264 + 8 * b])
                if b < 7:
                    mark(ins)
            ins.then_inc(S["pcz"], 1)
            settle()
            mark(dve.tensor_tensor(impD[0:16], impD[0:16], C("force0", rows=16), ALU.add))
            mark(dve.scalar_tensor_tensor(rowb[0:16].rearrange("p (n c) -> p n c", c=2),
                                          ptf[0:16, 96:128].unsqueeze(2).broadcast_to([16, 32, 2]), 32.0,
                                          C("selbase", rows=16).rearrange("p (n c) -> p n c", c=2), ALU.mult, ALU.add))
            settle()
            mark(dve.max(m16[0:16, 0:8], impD[0:16]))
            settle()
            mark(dve.max_index(i16[0:16, 0:8], m16[0:16, 0:8], impD[0:16]))
            mark(dve.match_replace(imp2[0:16], m16[0:16, 0:8], impD[0:16], -FORCE))
            settle()
            mark(dve.max(m16[0:16, 8:16], imp2[0:16]))
            settle()
            mark(dve.max_index(i16[0:16, 8:16], m16[0:16, 8:16], imp2[0:16]))
            settle()
            mark(dve.tensor_copy(f16[0:16], i16[0:16, :]))
            settle()
            onehot = tmpA[0:16, 0:1024].rearrange("p (s n) -> p s n", s=16)
            mark(dve.tensor_tensor(onehot, C("iota64", rows=16).unsqueeze(1).broadcast_to([16, 16, 64]),
                                   f16[0:16].unsqueeze(2).broadcast_to([16, 16, 64]), ALU.is_equal))
            settle()
            mark(dve.tensor_tensor(onehot, onehot, rowb[0:16].unsqueeze(1).broadcast_to([16, 16, 64]), ALU.mult))
            settle()
            dve.tensor_reduce(R16[0:16], onehot, AX_X, ALU.add).then_inc(S["r16"], 1)

            job_landed(dve, J_W2)
            ropeT = job(J_W2)[:, 3072:3072 + TOK]
            for h in range(8):
                dve.wait_ge(S["qm_ps"], h + 1)
                bk = bank[[3, 0, 1, 4][h % 4]]
                mark(dve.scalar_tensor_tensor(tA[64:96], bk[64:96, :], MLA_SCALE, ropeT[64:96, 0:SEQ], ALU.mult, ALU.mult))
                mark(dve.scalar_tensor_tensor(tB[64:96], bk[96:128, :], MLA_SCALE, ropeT[96:128, 0:SEQ], ALU.mult, ALU.mult))
                settle()
                dve.tensor_tensor(qmT[64:96, h * 512:(h + 1) * 512], tA[64:96], tB[64:96], ALU.add).then_inc(S["qm_dve"], 1)
                dve.wait_ge(S["qm_dve"], h + 1)
            dve.wait_ge(S["qmd_ps"], 1)

            def rt8(rows):
                return ropeT[rows, SEQ:TOK].unsqueeze(1).broadcast_to([32, 8, 8])

            def hb(ap):
                return ap.rearrange("p (h b) -> p h b", h=8)

            mark(dve.scalar_tensor_tensor(hb(tA[64:96, 0:64]), hb(bank[6][64:96, 64:128]), MLA_SCALE, rt8(slice(64, 96)), ALU.mult, ALU.mult))
            mark(dve.scalar_tensor_tensor(hb(tB[64:96, 0:64]), hb(bank[6][96:128, 64:128]), MLA_SCALE, rt8(slice(96, 128)), ALU.mult, ALU.mult))
            settle()
            dve.tensor_tensor(qmd[64:96], tA[64:96, 0:64], tB[64:96, 0:64], ALU.add).then_inc(S["qmd"], 1)
            dve.wait_ge(S["qmd"], 2)
            mark(dve.tensor_copy(kmT[64:96, 512:4096].rearrange("p (h c) -> p h c", h=7), kmT[64:96, 0:512].unsqueeze(1).broadcast_to([32, 7, 512])))
            dve.wait_ge(S["jobs_used"], J_WIN)
            for ck in range(2):
                mark(dve.tensor_copy(QL[:, ck * 256:(ck + 1) * 256].rearrange("p (b c) -> p b c", b=8)[:, :, 0:8],
                                     bank[6][:, P + ck * 64:P + (ck + 1) * 64].rearrange("p (h b) -> p b h", h=8)))
            dve.wait_ge(S["r16T_ps"], 1)
            dve.tensor_copy(RT16[0:16], bank[5][0:16, 0:16]).then_inc(S["rt16"], 1)
            dve.wait_ge(S["idxs_ps"], 1)
            ts(idxi[:, 96:112], bank[5][:, 16:32], C("mod", 2, 1), ALU.add).then_inc(S["idxs"], 1)
            dve.wait_ge(S["ocd_ps"], 1)
            mark(ts(oC64[0:64], bank[5][0:64, 384:448], C("ggrp", 0, 1, rows=64), ALU.mult))
            settle()
            mark(dve.scalar_tensor_tensor(oC64[0:64], bank[5][0:64, 448:512], C("ggrp", 1, 1, rows=64), oC64[0:64], ALU.mult, ALU.add))
            settle()
            mark(ts(oC64[0:64], oC64[0:64], g3[0:64, 0:1], ALU.mult))
            dve.wait_ge(S["pcpT_ps"], 1)
            dve.tensor_copy(Sc, bank[1][:, :]).then_inc(S["pcpT"], 1)
            settle()
            for tl in range(TILES):
                dve.wait_ge(S["ocp_ps"], tl + 1)
                mark(dve.tensor_copy(OA[:, tl * 512:(tl + 1) * 512], bank[[2, 3, 0, 4][tl]][:, :]))
            dve.wait_ge(S["kv_stored"], 1)
            settle()
            mark(dve.memset(QZs, 0.0))
            mark(dve.memset(QR, 0.0))
            settle()
            for s2 in range(2):
                for g in range(2):
                    for e in range(2):
                        dst = QZs[64 * s2:64 * s2 + 64].rearrange("p (b g s c) -> p b g s c", b=8, g=2, s=2)[:, :, g, s2, e:e + 3:2]
                        src = bank[7][64 * e:64 * e + 64, P + 8 * (4 + 2 * g):P + 8 * (6 + 2 * g)].rearrange("p (k b) -> p b k", k=2)
                        mark(ts(dst, src, NSA_SCALE, ALU.mult))
            dve.wait_ge(S["qmd"], 2)
            for v in range(4):
                dst = QR[32 * v:32 * v + 32].rearrange("p (b v c) -> p b v c", b=8, v=4)[:, :, v, 0:8]
                mark(dve.tensor_copy(dst, qmd[64:96].rearrange("p (h b) -> p b h", h=8)))
            settle()
            dve.engine_nop().then_inc(S["xg_dead"], 1)
            dve.engine_nop().then_inc(S["prep_dve"], 1)

            def unit_max(u):
                _, _, tl = unit(u)
                dve.wait_ge(S["s"], u + 1)
                dve.tensor_reduce(NMp[:, u:u + 1], bank[u % 2][:, 0:(tl + 1) * P], AX_X, ALU.max, negate=True).then_inc(S["nm"], 1)

            def pt_copy(u):
                _, _, tl = unit(u)
                dve.wait_ge(S["pt_ps"], u + 1)
                if u >= 2:
                    dve.wait_ge(S["o_ps"], u - 1)
                dve.tensor_copy(PTb[u % 2][:, 0:(tl + 1) * P], bank[2 + u % 2][:, 0:(tl + 1) * P]).then_inc(S["pt_by_V"], 1)

            def fold(u):
                br, h, tl = unit(u)
                dve.wait_ge(S["p"], u + 1)
                mark(dve.reciprocal(CFp[:, u:u + 1], RSp[:, u:u + 1]))
                settle()
                if br < 2:
                    g = tl * 24 + h * 3 + 1 + br
                    mark(dve.tensor_tensor(CFp[:, u:u + 1], CFp[:, u:u + 1], gsig[:, g:g + 1], ALU.mult))
                    settle()
                dve.wait_ge(S["o_ps"], u + 1)
                at = tl * 512 + h * 64
                if br < 2:
                    if br == 1:
                        dve.wait_ge(S["o"], h * 4 + tl + 1)
                    dve.scalar_tensor_tensor(OA[:, at:at + 64], bank[4][:, 0:64], CFp[:, u:u + 1], OA[:, at:at + 64], ALU.mult, ALU.add).then_inc(S["o"], 1)
                else:
                    ts(OB[:, at:at + 64], bank[4][:, 0:64], CFp[:, u:u + 1], ALU.mult).then_inc(S["o"], 1)

            def dec_max(c):
                n, w = c["n"], c["width"]
                dve.wait_ge(S["ds"], n + 1)
                if c["part"] == "new":
                    name = {"win": "newW", "slc": "newS", "mla": "newM"}[c["kind"]]
                    mark(dve.tensor_tensor(bank[5][:, 0:8], bank[5][:, 0:8], C(name, c["r"] * 8, 8), ALU.add))
                    settle()
                elif c["kind"] == "slc":
                    mark(dve.memset(bank[5][:, :].rearrange("p (a c) -> p a c", a=4)[:, :, 120:128], NEG))
                    settle()
                ins = dve.tensor_reduce(NMd[:, n:n + 1], bank[5][:, 0:w], AX_X, ALU.max, negate=True)
                if not c["first"]:
                    mark(ins)
                    settle()
                    ins = dve.tensor_tensor(NMd[:, n:n + 1], NMd[:, n:n + 1], NMd[:, n - 1:n], ALU.min)
                ins.then_inc(S["dnm"], 1)

            def dt_copy(st):
                m = use_of[st]
                if dt_use[m] != "V":
                    return
                dve.wait_ge(S["dt_ps"], m + 1)
                if st[0] == "K":
                    before = sum(1 for x in steps[:steps.index(st)] if x[0] == "C")
                    if before:
                        dve.wait_ge(S["ds"], before)
                    dve.tensor_copy(KTs[:, st[2] * 512:(st[2] + 1) * 512], bank[6][:, :]).then_inc(S["dt_by_V"], 1)
                else:
                    c = chunks[st[1]]
                    if c["n"] >= 1:
                        dve.wait_ge(S["do_ps"], c["n"])
                    k = DEC if c["part"] == "new" else P
                    dve.tensor_copy(PTd[0:k, 0:c["blocks"] * P], bank[6][0:k, 0:c["blocks"] * P]).then_inc(S["dt_by_V"], 1)

            def dec_fold(c):
                n, pv, r = c["n"], c["pv"], c["r"]
                out = {"win": owW, "slc": owS, "mla": OF}[c["kind"]][:, r * pv:(r + 1) * pv]
                dve.wait_ge(S["dp"], n + 1)
                if c["first"]:
                    mark(dve.tensor_copy(LD[:, n:n + 1], RSd[:, n:n + 1]))
                    dve.wait_ge(S["do_ps"], n + 1)
                    dve.tensor_copy(out, bank[7][:, 0:pv]).then_inc(S["do"], 1)
                else:
                    dve.wait_ge(S["do"], n)
                    settle()
                    mark(dve.scalar_tensor_tensor(LD[:, n:n + 1], LD[:, n - 1:n], ALd[:, n:n + 1], RSd[:, n:n + 1], ALU.mult, ALU.add))
                    dve.wait_ge(S["do_ps"], n + 1)
                    dve.scalar_tensor_tensor(out, out, ALd[:, n:n + 1], bank[7][:, 0:pv], ALU.mult, ALU.add).then_inc(S["do"], 1)
                if c["last"] and c["kind"] != "mla":
                    settle()
                    dve.wait_ge(S["do"], n + 1)
                    mark(dve.reciprocal(lnv[:, n % 16:n % 16 + 1], LD[:, n:n + 1]))
                    settle()
                    mark(ts(out, out, lnv[:, n % 16:n % 16 + 1], ALU.mult))

            prev = None
            for u in range(UNITS + 3):
                st = steps[u - FIRST_STEP] if FIRST_STEP <= u < FIRST_STEP + len(steps) else None
                if prev is not None:
                    dt_copy(("T", prev["n"]))
                if u < UNITS:
                    unit_max(u)
                if st is not None and st[0] == "K":
                    dt_copy(st)
                if st is not None and st[0] == "C":
                    dec_max(chunks[st[1]])
                if 2 <= u < UNITS + 2 and pt_by(u - 2) == "V":
                    pt_copy(u - 2)
                if u >= 3:
                    fold(u - 3)
                if prev is not None:
                    dec_fold(prev)
                prev = chunks[st[1]] if st is not None and st[0] == "C" else None

            settle()
            dve.wait_ge(S["do"], len(chunks))
            lo = next(c["n"] for c in chunks if c["kind"] == "mla") + 4
            mark(dve.tensor_copy(mrg[:, 0:8], NMd[:, lo:lo + 36:5]))
            mark(dve.tensor_copy(mrg[:, 8:16], LD[:, lo:lo + 36:5]))
            for r in range(2):
                mark(ts(mrg[:, 320 + r * 64:384 + r * 64], owW[:, r * P:r * P + 64], C("ggrp32", 0, 1), ALU.mult))
            settle()
            for r in range(2):
                ins = dve.scalar_tensor_tensor(mrg[:, 320 + r * 64:384 + r * 64], owW[:, r * P + 64:(r + 1) * P], C("ggrp32", 1, 1),
                                               mrg[:, 320 + r * 64:384 + r * 64], ALU.mult, ALU.add)
                if r == 0:
                    mark(ins)
            ins.then_inc(S["mrg"], 1)
            dve.wait_ge(S["x2_in"], 16)
            for k in range(KM):
                ts(XG[:, k * TOK:(k + 1) * TOK], XG[:, k * TOK:(k + 1) * TOK], normpre[:, k:k + 1], ALU.mult).then_inc(S["xg2"], 1)
            dve.wait_ge(S["mrg_ps"], 1)

            def parts(ap):
                return ap.rearrange("p (j h) -> p h j", j=4)

            def heads(ap):
                return ap.unsqueeze(1).broadcast_to([8, 4, 32])

            def jh(ap):
                return ap.rearrange("p (j h) -> p j h", j=4)

            low = mrg[0:8, 144:176]
            mark(dve.tensor_reduce(low, parts(bank[5][0:8, 0:P]), AX_X, ALU.min))
            settle()
            dve.tensor_tensor(jh(Pd[0:8, 0:P]), heads(low), jh(bank[5][0:8, 0:P]), ALU.subtract).then_inc(S["mrg_d"], 1)
            dve.wait_ge(S["mrg_e"], 1)
            mark(dve.tensor_tensor(Pd[0:8, 256:384], Pd[0:8, P:256], bank[5][0:8, P:256], ALU.mult))
            settle()
            mark(dve.tensor_reduce(Pd[0:8, 384:416], parts(Pd[0:8, 256:384]), AX_X, ALU.add))
            settle()
            mark(dve.reciprocal(Pd[0:8, 416:448], Pd[0:8, 384:416]))
            settle()
            dve.tensor_tensor(jh(mrg[0:8, 16:16 + P]), jh(Pd[0:8, P:256]), heads(Pd[0:8, 416:448]), ALU.mult).then_inc(S["coef"], 1)
            dve.wait_ge(S["ob_ps"], 1)
            mark(dve.scalar_tensor_tensor(od1[0:64], bank[7][0:64, 0:64], g3[0:64, 1:2], oC64[0:64], ALU.mult, ALU.add))
            settle()
            dve.scalar_tensor_tensor(od1[0:64], bank[7][0:64, 64:128], g3[0:64, 2:3], od1[0:64], ALU.mult, ALU.add).then_inc(S["oa64"], 1)
            dve.wait_ge(S["coef_ps"], 1)
            mark(dve.tensor_copy(coefT[:, 0:8], bank[5][:, 256:264]))
            settle()
            dve.tensor_tensor(Wsel.rearrange("p (b h) -> p b h", b=8), coefT[:, 0:8].unsqueeze(2).broadcast_to([P, 8, 8]),
                              C("selH").unsqueeze(1).broadcast_to([P, 8, 8]), ALU.mult).then_inc(S["wsel"], 1)
            dve.wait_ge(S["oad_ps"], 1)
            mark(dve.tensor_copy(OA[0:DEC, 2048:2560], bank[4][0:DEC, :]))
            dve.wait_ge(S["olat_ps"], 1)
            for ck in range(2):
                ins = dve.tensor_copy(mrg[:, 192 + ck * 64:256 + ck * 64].rearrange("p (h b) -> p b h", h=8),
                                      bank[6][:, ck * 64:(ck + 1) * 64].rearrange("p (b h) -> p b h", b=8))
                if ck == 0:
                    mark(ins)
            ins.then_inc(S["olat"], 1)
            dve.wait_ge(S["obd_ps"], 1)
            mark(dve.tensor_copy(OB[0:DEC, 2048:2560], bank[5][0:DEC, :]))
            settle()

            n_sg = n_sig = 0
            for v, (kind, n, x, half) in enumerate(ztiles):
                m = P if x < TILES else DEC
                bk = bank[v % 4]
                if z_by(v) == "dve":
                    dve.wait_ge(S["z_ps"], v + 1)
                if kind == "silu":
                    n_sg += 1
                    dve.wait_ge(S["sg"], n_sg)
                    o = (OA if n == J_GA else OB)[0:m, x * 512:(x + 1) * 512]
                    q = ((n_sg - 1) % 2) * 512
                    if n_sg > 1:
                        dve.wait_ge(S["gated"], n_sg - 1)
                    dve.scalar_tensor_tensor(ztmp[0:m, 0:512], bk[0:m, :], rs5[0:m, x:x + 1], sA[0:m, q:q + 512], ALU.mult, ALU.mult).then_inc(S["z_by_dve"], 1)
                    z_free(dve, v)
                    dve.tensor_tensor(o, o, ztmp[0:m, 0:512], ALU.mult).then_inc(S["gated"], 1)
                elif kind in ("oT", "hT") and z_by(v) == "dve":
                    dve.tensor_copy((oT if kind == "oT" else hT)[:, x * TOK:x * TOK + SEQ], bk[:, :]).then_inc(S["z_by_dve"], 1)
                elif kind in ("oTd", "hTd"):
                    dst = (oT if kind == "oTd" else hT).rearrange("p (k t) -> p k t", k=8)[:, :, SEQ:TOK]
                    dve.tensor_copy(dst, bk[:, 0:64].rearrange("p (k t) -> p k t", k=8)).then_inc(S["z_by_dve"], 1)
                elif kind == "pa":
                    if x == 0:
                        z_free(dve, v - 1)
                        z_free(dve, v - 6)
                    at = x * D_MODEL + half * 512
                    dve.tensor_tensor(H[0:m, at:at + 512], sA[0:m, x * 512:(x + 1) * 512], bk[0:m, :], ALU.mult).then_inc(S["z_by_dve"], 1)
                elif kind == "pb":
                    at = x * D_MODEL + half * 512
                    if x or half:
                        dve.wait_ge(S["h"], 5 * half + x)
                    dve.tensor_tensor(ztmp[0:m, 0:512], sB[0:m, x * 512:(x + 1) * 512], bk[0:m, :], ALU.mult).then_inc(S["z_by_dve"], 1)
                    z_free(dve, v)
                    dve.tensor_tensor(H[0:m, at:at + 512], H[0:m, at:at + 512], ztmp[0:m, 0:512], ALU.add).then_inc(S["h"], 1)
                elif kind == "wo":
                    at = x * D_MODEL + half * 512
                    dve.tensor_copy(H[0:m, at:at + 512], bk[0:m, :]).then_inc(S["z_by_dve"], 1)
                    dve.engine_nop().then_inc(S["zc"], 1)
            dve.wait_ge(S["sqz"], 10)
            mark(dve.tensor_reduce(vz, ssz.rearrange("p (t c) -> p t c", c=2), AX_X, ALU.add))
            settle()
            ts(vz, vz, 1.0 / D_MODEL, ALU.mult, EPS, ALU.add).then_inc(S["vz"], 1)
            dve.wait_ge(S["vz"], 1)
            dve.wait_ge(S["rtz"], 1)
            root_inverse(rsz, vz, rtz, tcol[:, 0:5], S["rsz"])
            dve.wait_ge(S["xend_in"], 48)
            z_free(dve, len(ztiles) - 1)
            for tl in range(5):
                m = P if tl < TILES else DEC
                y = H[0:m, tl * D_MODEL:(tl + 1) * D_MODEL]
                x = job(N_JOBS)[:, tl * D_MODEL:(tl + 1) * D_MODEL] if tl < TILES else OA[0:DEC, 0:D_MODEL]
                mark(dve.scalar_tensor_tensor(y, y, rsz[0:m, tl:tl + 1], OB[0:m, 0:D_MODEL], ALU.mult, ALU.mult))
                settle()
                dve.tensor_tensor(y, y, x, ALU.add).then_inc(S["y"], 1)


def kernel(x_prompt, x_sample, cache_nsa_cmp, cache_nsa_slc, cache_mla_latent, cache_mla_krope, state_nsa_win,
           page_table, norm_pre, w_in, pe_cmp, q_norm, w_q_up, kv_norm, w_kv_up, w_proj_a, w_proj_b, w_out, norm_post):
    import numpy as _np
    import concourse.bacc as _bacc
    from concourse import mybir as _mybir
    from concourse.bass_utils import run_bass_kernel_spmd as _run

    A = _np.asarray
    n_phys = cache_nsa_cmp.shape[1]
    x = _np.concatenate([A(x_prompt)[0], A(x_sample)[:, 0]], 0)
    w = A(w_in)[0]
    cuts = _np.cumsum([512, 256, 256, 256, 24, 512, Q_LORA, KV_LORA, ROPE_D, 512, D_MODEL, D_MODEL])[:-1]
    qa, kvc, kvs, kvw, gn, ga, qd, kvd, krp, gb, ma, mb = _np.split(w, cuts, axis=1)

    def kv_split(a):
        a = a.reshape(D_MODEL, KVH, 2, HD)
        return a[:, :, 0].reshape(D_MODEL, -1), a[:, :, 1].reshape(D_MODEL, -1)

    (kc, vc), (ks, vs), (kw, vw) = kv_split(kvc), kv_split(kvs), kv_split(kvw)
    w_attn = _np.concatenate([qa, ks, kw, vs, vw, kc, vc, gn, qd, kvd, krp], axis=1)

    def by_chunk(a, groups):
        k, c = a.shape[0] // P, a.shape[1] // groups
        return a.reshape(k, P, groups, c).transpose(1, 2, 0, 3).reshape(P, groups, k * c)

    w_gate = _np.concatenate([ga, gb, ma, mb], axis=1)
    qup = A(w_q_up)[0]
    pe_part = qup[:, :, NOPE:]
    swapped = _np.concatenate([pe_part[..., 16:], pe_part[..., :16]], -1)
    qup = _np.concatenate([qup, swapped], -1).reshape(3, P, 8 * P).transpose(1, 0, 2).reshape(P, -1)
    kup = A(w_kv_up)[0]
    w_k = kup[:, :, :NOPE].reshape(2, P, 512).transpose(1, 0, 2).reshape(P, -1)
    w_v = kup[:, :, NOPE:].reshape(2, P, 512).transpose(1, 0, 2).reshape(P, -1)
    w_kT = kup[:, :, :NOPE].transpose(2, 1, 0).reshape(NOPE, -1)
    pt = A(page_table)
    cmp_ = A(cache_nsa_cmp)[0].transpose(0, 1, 3, 2, 4).reshape(n_phys * 16, 8 * 256)
    slc = A(cache_nsa_slc)[0].reshape(n_phys, 2, 8, 8, KVH, 2, HD).transpose(0, 1, 4, 2, 5, 3, 6).reshape(n_phys * 32, 1024)
    lat = A(cache_mla_latent)[0]
    latT = lat.reshape(n_phys, PAGE, 2, P).transpose(0, 3, 2, 1).reshape(n_phys, P, 256)
    krT = A(cache_mla_krope)[0].transpose(0, 2, 1).reshape(n_phys * 32, P)
    arrays = {
        "x": x, "xT": x.T.reshape(KM, P, TOK).transpose(1, 0, 2).reshape(P, -1),
        "norm_pre": A(norm_pre)[0].reshape(KM, P).T, "q_norm": A(q_norm)[0].reshape(3, P).T,
        "kv_norm": A(kv_norm).reshape(1, -1), "norm_post": A(norm_post).reshape(1, -1),
        "w_attn": w_attn.reshape(KM, P, W_ATTN).transpose(1, 0, 2),
        "w_gate": by_chunk(w_gate, 6), "w_qup": qup, "w_k": w_k, "w_v": w_v, "w_kT": w_kT,
        "w_pa": by_chunk(A(w_proj_a)[0], 2), "w_pb": by_chunk(A(w_proj_b)[0], 2), "w_out": by_chunk(A(w_out)[0], 2),
        "pe": A(pe_cmp)[0].transpose(0, 2, 1, 3).reshape(CMP_BLOCK, 256),
        "cmp": cmp_, "slc": slc, "krT": krT,
        "latent": _np.concatenate([lat, latT], -1),
        "win": A(state_nsa_win)[0].transpose(0, 1, 3, 2, 4).reshape(DEC, WINDOW, 256),
        "pt8": pt.reshape(32, 8).T, "pt4": pt.reshape(64, 4).T, "pt16": _np.repeat(pt, 2, axis=0), "ptflat": pt.reshape(1, -1),
        "const": CONST,
    }
    outs = {"o_y": (TOK, D_MODEL), "o_kv": (TOK, 768), "o_c": (TOK, KV_LORA), "o_kr": (TOK, ROPE_D), "o_win": (DEC, WINDOW, 256)}
    nc = _bacc.Bacc("TRN2", target_bir_lowering=False, num_devices=1)
    arrays = {k: _np.ascontiguousarray(v) for k, v in arrays.items()}
    t = {k: nc.dram_tensor(k, v.shape, _mybir.dt.from_np(v.dtype), kind="ExternalInput").ap() for k, v in arrays.items()}
    t.update({k: nc.dram_tensor(k, s, F32, kind="ExternalOutput").ap() for k, s in outs.items()})
    build(nc, t)
    r = _run(nc, [arrays], core_ids=[0]).results[0]
    y, kv, c, kr, win = (_np.asarray(r[k]) for k in ("o_y", "o_kv", "o_c", "o_kr", "o_win"))

    def cache(k, v):
        return _np.stack([k.reshape(-1, KVH, HD), v.reshape(-1, KVH, HD)], axis=2)

    slc_n, win_n, cmp_n = cache(kv[:, 0:128], kv[:, 256:384]), cache(kv[:, 128:256], kv[:, 384:512]), cache(kv[:, 512:640], kv[:, 640:768])
    win_s = win.reshape(DEC, WINDOW, 2, KVH, HD).transpose(0, 1, 3, 2, 4)

    def p_(a):
        return a[None, None, :SEQ]

    def s_(a):
        return a[None, SEQ:, None]

    return (y[None, :SEQ], y[SEQ:, None], p_(cmp_n), p_(slc_n), p_(c), p_(kr), p_(win_n),
            s_(cmp_n), s_(slc_n), s_(c), s_(kr), _np.ascontiguousarray(win_s)[None])
```
